# Optimizing a Trainium2 kernel written in Bass

```python
import math
import jax, jax.numpy as jnp
from jax import lax
import numpy as np

D_MODEL = 1024
BATCH = 1
SEQ = 512
DEPTH = 1

CHUNK = 64
QBLOCK = 128
PEER_BLOCK = 128

D_MIX = D_MODEL
SSD_WIDTH = D_MIX // 2
SSD_HEAD_DIM = 64
SSD_HEADS = SSD_WIDTH // SSD_HEAD_DIM
SSD_GROUPS = 2
SSD_HPG = SSD_HEADS // SSD_GROUPS
SSD_STATE = 128
SSD_CONV = 4
SSD_CONV_CH = SSD_WIDTH + 2 * SSD_GROUPS * SSD_STATE

DIFF_WIDTH = D_MIX - SSD_WIDTH
DIFF_HEAD_DIM = 64
DIFF_HEADS = DIFF_WIDTH // (2 * DIFF_HEAD_DIM)
ROPE_THETA = 10000.0

IN_WIDTH = SSD_WIDTH + SSD_CONV_CH + SSD_HEADS + 3 * DIFF_WIDTH

PEER_HEADS = 8
PEER_NKEYS = 128
PEER_EXPERTS = PEER_NKEYS * PEER_NKEYS
PEER_TOPK = 16
PEER_QDIM = 256
PEER_HALF = PEER_QDIM // 2

PLE_DIM = 256
EPS = 1e-6

kernel_name = "hybrid_ssd_diffattn_peer_block"

def rms_norm(x, g):
    xf = x.astype(jnp.float32)
    y = xf * lax.rsqrt(jnp.mean(xf * xf, axis=-1, keepdims=True) + EPS)
    return (y * g.astype(jnp.float32)).astype(x.dtype)

def causal_depthwise_conv(u, w, b):
    out = lax.conv_general_dilated(
        u, w[:, None, :].astype(u.dtype), window_strides=(1,),
        padding=[(w.shape[0] - 1, 0)],
        dimension_numbers=("NWC", "WIO", "NWC"),
        feature_group_count=u.shape[-1])
    return out + b.astype(u.dtype)

def ssd_mixer(z, xbc, dt_raw, conv_w, conv_b, dt_bias, a_log, d_skip, norm_g):
    b, L, _ = z.shape
    nc = L // CHUNK
    xbc = jax.nn.silu(causal_depthwise_conv(xbc, conv_w, conv_b))
    xs, bm, cm = jnp.split(xbc, [SSD_WIDTH, SSD_WIDTH + SSD_GROUPS * SSD_STATE], axis=-1)
    xs = xs.reshape(b, nc, CHUNK, SSD_GROUPS, SSD_HPG, SSD_HEAD_DIM)
    bm = bm.reshape(b, nc, CHUNK, SSD_GROUPS, SSD_STATE)
    cm = cm.reshape(b, nc, CHUNK, SSD_GROUPS, SSD_STATE)
    dt = jax.nn.softplus(dt_raw.astype(jnp.float32) + dt_bias.astype(jnp.float32))
    dt = dt.reshape(b, nc, CHUNK, SSD_GROUPS, SSD_HPG)
    a = -jnp.exp(a_log.astype(jnp.float32)).reshape(SSD_GROUPS, SSD_HPG)
    a_cs = jnp.cumsum(dt * a, axis=2)
    xdt = xs * dt[..., None]

    tri = jnp.tril(jnp.ones((CHUNK, CHUNK), dtype=bool))[:, :, None, None]
    seg = a_cs[:, :, :, None] - a_cs[:, :, None, :]
    lmat = jnp.exp(jnp.where(tri, seg, -jnp.inf))
    cb = jnp.einsum("bclgn,bcsgn->bclsg", cm, bm)
    y_diag = jnp.einsum("bclsg,bclsgr,bcsgrp->bclgrp", cb, lmat, xdt)

    decay_states = jnp.exp(a_cs[:, :, -1:] - a_cs)
    states = jnp.einsum("bclgn,bclgr,bclgrp->bcgrpn", bm, decay_states, xdt)
    chunk_decay = jnp.exp(a_cs[:, :, -1])

    def step(carry, inp):
        st, dec = inp
        return carry * dec[..., None, None] + st, carry

    init = jnp.zeros((b, SSD_GROUPS, SSD_HPG, SSD_HEAD_DIM, SSD_STATE), states.dtype)
    _, prev = lax.scan(step, init, (jnp.moveaxis(states, 1, 0), jnp.moveaxis(chunk_decay, 1, 0)))
    prev = jnp.moveaxis(prev, 0, 1)
    y_off = jnp.einsum("bclgn,bcgrpn,bclgr->bclgrp", cm, prev, jnp.exp(a_cs))

    y = y_diag + y_off + d_skip.reshape(SSD_GROUPS, SSD_HPG, 1) * xs
    y = y.reshape(b, L, SSD_WIDTH).astype(z.dtype)
    yg = (y * jax.nn.silu(z)).reshape(b, L, SSD_GROUPS, SSD_WIDTH // SSD_GROUPS)
    yg = rms_norm(yg, norm_g.reshape(SSD_GROUPS, -1))
    return yg.reshape(b, L, SSD_WIDTH)

def rope(x, cos, sin):
    half = x.shape[-1] // 2
    c = cos[:, :, None, None, :]
    s = sin[:, :, None, None, :]
    xf = x.astype(jnp.float32)
    x1, x2 = xf[..., :half], xf[..., half:]
    return jnp.concatenate([x1 * c - x2 * s, x2 * c + x1 * s], axis=-1).astype(x.dtype)

def diff_attention(q, k, v, positions, q_norm_g, k_norm_g, lam_vecs, out_norm_g, lam_init):
    b, L, _ = q.shape
    q = q.reshape(b, L, DIFF_HEADS, 2, DIFF_HEAD_DIM)
    k = k.reshape(b, L, DIFF_HEADS, 2, DIFF_HEAD_DIM)
    v = v.reshape(b, L, DIFF_HEADS, 2 * DIFF_HEAD_DIM)
    inv_freq = 1.0 / (ROPE_THETA ** (jnp.arange(0, DIFF_HEAD_DIM, 2, dtype=jnp.float32) / DIFF_HEAD_DIM))
    ang = positions[..., None].astype(jnp.float32) * inv_freq
    cos, sin = jnp.cos(ang), jnp.sin(ang)
    q = rope(rms_norm(q, q_norm_g), cos, sin)
    k = rope(rms_norm(k, k_norm_g), cos, sin)
    lv = lam_vecs.astype(jnp.float32)
    lam = jnp.exp(jnp.sum(lv[0] * lv[1])) - jnp.exp(jnp.sum(lv[2] * lv[3])) + lam_init
    scale = DIFF_HEAD_DIM ** -0.5
    outs = []
    for blk in range(L // QBLOCK):
        q0 = blk * QBLOCK
        kend = q0 + QBLOCK
        s = jnp.einsum("bqhcd,bkhcd->bhcqk", q[:, q0:kend], k[:, :kend]).astype(jnp.float32) * scale
        q_chunk = (q0 + jnp.arange(QBLOCK)) // CHUNK
        k_chunk = jnp.arange(kend) // CHUNK
        mask = k_chunk[None, :] <= q_chunk[:, None]
        probs = jax.nn.softmax(jnp.where(mask, s, -jnp.inf), axis=-1)
        attn = probs[:, :, 0] - lam * probs[:, :, 1]
        outs.append(jnp.einsum("bhqk,bkhe->bqhe", attn.astype(v.dtype), v[:, :kend]))
    o = jnp.concatenate(outs, axis=1)
    o = rms_norm(o, out_norm_g) * (1.0 - lam_init)
    return o.reshape(b, L, DIFF_WIDTH)

def peer_ffn(xn, wq, sub_k1, sub_k2, expert_u, expert_v):
    b, L, d = xn.shape
    xb = xn.reshape((b * L) // PEER_BLOCK, PEER_BLOCK, d)

    def block(xt):
        q = (xt @ wq).reshape(PEER_BLOCK, PEER_HEADS, 2, PEER_HALF)
        s1 = jnp.einsum("thd,kd->thk", q[:, :, 0], sub_k1).astype(jnp.float32)
        s2 = jnp.einsum("thd,kd->thk", q[:, :, 1], sub_k2).astype(jnp.float32)
        v1, i1 = lax.top_k(s1, PEER_TOPK)
        v2, i2 = lax.top_k(s2, PEER_TOPK)
        cand = (v1[..., :, None] + v2[..., None, :]).reshape(PEER_BLOCK, PEER_HEADS, PEER_TOPK * PEER_TOPK)
        cidx = (i1[..., :, None] * PEER_NKEYS + i2[..., None, :]).reshape(PEER_BLOCK, PEER_HEADS, PEER_TOPK * PEER_TOPK)
        top, pos = lax.top_k(cand, PEER_TOPK)
        eidx = jnp.take_along_axis(cidx, pos, axis=-1)
        g = jax.nn.softmax(top, axis=-1)
        u = expert_u[eidx]
        act = jax.nn.gelu(jnp.einsum("td,thkd->thk", xt, u), approximate=False)
        w = (act.astype(jnp.float32) * g).astype(xt.dtype)
        return jnp.einsum("thk,thkd->td", w, expert_v[eidx])

    return lax.map(block, xb).reshape(b, L, d)

def setup_inputs(seed: int = 0) -> dict:
    key = jax.random.key(seed)
    ks = jax.random.split(key, 32)

    def nrm(k, shape, scale):
        return jax.random.normal(k, shape, jnp.float32) * scale

    def gain(k, shape):
        return 1.0 + 0.05 * jax.random.normal(k, shape, jnp.float32)

    x = jax.random.normal(ks[0], (BATCH, SEQ, D_MODEL), jnp.float32)
    p = jax.random.normal(ks[1], (DEPTH, BATCH, SEQ, PLE_DIM), jnp.float32)
    offsets = jax.random.randint(ks[2], (BATCH, 1), 0, 64, dtype=jnp.int32) * CHUNK
    positions = (offsets + jnp.arange(SEQ, dtype=jnp.int32)[None, :]).astype(jnp.int32)

    dt = jnp.exp(jax.random.uniform(ks[3], (DEPTH, SSD_HEADS), jnp.float32)
                 * (math.log(0.1) - math.log(0.001)) + math.log(0.001))
    dt_bias = dt + jnp.log(-jnp.expm1(-dt))
    a_log = jnp.log(jax.random.uniform(ks[4], (DEPTH, SSD_HEADS), jnp.float32, 1.0, 16.0))

    return {
        "x": x,
        "p": p,
        "positions": positions,
        "norm_mix_g": gain(ks[5], (DEPTH, D_MODEL)),
        "w_in": nrm(ks[6], (DEPTH, D_MODEL, IN_WIDTH), D_MODEL ** -0.5),
        "conv_w": nrm(ks[7], (DEPTH, SSD_CONV, SSD_CONV_CH), SSD_CONV ** -0.5),
        "conv_b": nrm(ks[8], (DEPTH, SSD_CONV_CH), 0.02),
        "dt_bias": dt_bias,
        "a_log": a_log,
        "d_skip": gain(ks[9], (DEPTH, SSD_HEADS)),
        "ssd_norm_g": gain(ks[10], (DEPTH, SSD_WIDTH)),
        "q_norm_g": gain(ks[11], (DEPTH, DIFF_HEAD_DIM)),
        "k_norm_g": gain(ks[12], (DEPTH, DIFF_HEAD_DIM)),
        "lam_vecs": nrm(ks[13], (DEPTH, 4, DIFF_HEAD_DIM), 0.1),
        "diff_norm_g": gain(ks[14], (DEPTH, 2 * DIFF_HEAD_DIM)),
        "w_out": nrm(ks[15], (DEPTH, D_MIX, D_MODEL), D_MIX ** -0.5),
        "norm_ffn_g": gain(ks[16], (DEPTH, D_MODEL)),
        "peer_wq": nrm(ks[17], (DEPTH, D_MODEL, PEER_HEADS * PEER_QDIM), D_MODEL ** -0.5),
        "peer_k1": nrm(ks[18], (DEPTH, PEER_NKEYS, PEER_HALF), PEER_HALF ** -0.5),
        "peer_k2": nrm(ks[19], (DEPTH, PEER_NKEYS, PEER_HALF), PEER_HALF ** -0.5),
        "peer_u": nrm(ks[20], (DEPTH, PEER_EXPERTS, D_MODEL), D_MODEL ** -0.5),
        "peer_v": nrm(ks[21], (DEPTH, PEER_EXPERTS, D_MODEL), (PEER_HEADS * PEER_TOPK) ** -0.5),
        "ple_proj": nrm(ks[22], (DEPTH, PLE_DIM, D_MODEL), PLE_DIM ** -0.5),
        "ple_norm_g": gain(ks[23], (DEPTH, D_MODEL)),
        "ple_gate_norm_g": gain(ks[24], (DEPTH, D_MODEL)),
        "ple_gate_w": nrm(ks[25], (DEPTH, D_MODEL, D_MODEL), D_MODEL ** -0.5),
    }

def reference(x, p, positions, norm_mix_g, w_in, conv_w, conv_b, dt_bias, a_log, d_skip,
              ssd_norm_g, q_norm_g, k_norm_g, lam_vecs, diff_norm_g, w_out, norm_ffn_g,
              peer_wq, peer_k1, peer_k2, peer_u, peer_v, ple_proj, ple_norm_g,
              ple_gate_norm_g, ple_gate_w):
    h = x
    splits = np.cumsum([SSD_WIDTH, SSD_CONV_CH, SSD_HEADS, DIFF_WIDTH, DIFF_WIDTH]).tolist()
    for i in range(DEPTH):
        lam_init = 0.8 - 0.6 * math.exp(-0.3 * i)
        n = rms_norm(h, norm_mix_g[i])
        z, xbc, dt_raw, q, k, v = jnp.split(n @ w_in[i], splits, axis=-1)
        y_ssd = ssd_mixer(z, xbc, dt_raw, conv_w[i], conv_b[i], dt_bias[i], a_log[i],
                          d_skip[i], ssd_norm_g[i])
        y_diff = diff_attention(q, k, v, positions, q_norm_g[i], k_norm_g[i], lam_vecs[i],
                                diff_norm_g[i], lam_init)
        h = h + jnp.concatenate([y_ssd, y_diff], axis=-1) @ w_out[i]
        h = h + peer_ffn(rms_norm(h, norm_ffn_g[i]), peer_wq[i], peer_k1[i], peer_k2[i],
                         peer_u[i], peer_v[i])
        e = rms_norm(p[i] @ ple_proj[i], ple_norm_g[i])
        gate = jax.nn.sigmoid(rms_norm(h, ple_gate_norm_g[i]) @ ple_gate_w[i])
        h = h + gate * e
    return h


_drawn_inputs = setup_inputs


def setup_inputs(seed=0):
    import zlib

    import numpy as np

    out = dict(_drawn_inputs(seed))
    spreads = {}
    factors = {'conv_b': 3.936,
     'd_skip': 3.077,
     'q_norm_g': 2.685,
     'k_norm_g': 2.988,
     'lam_vecs': 8.0,
     'diff_norm_g': 2.814,
     'norm_ffn_g': 7.524,
     'ple_norm_g': 3.12,
     'ple_gate_norm_g': 7.892}
    for name, (base, spread) in spreads.items():
        noise = np.random.default_rng([zlib.crc32(name.encode()), seed]).standard_normal(out[name].shape)
        drawn = base * np.exp(spread * noise) if base else spread * noise
        out[name] = __import__('jax').numpy.asarray(drawn.astype(out[name].dtype))
    for name, factor in factors.items():
        out[name] = (out[name] * factor).astype(out[name].dtype)
    return out
```

```python
import math
from contextlib import ExitStack

import numpy as np

import concourse.bass as bass
from concourse import mybir

F32 = mybir.dt.float32
F32R = mybir.dt.float32r
I32 = mybir.dt.int32
U32 = mybir.dt.uint32
ALU = mybir.AluOpType
ACT = mybir.ActivationFunctionType
AX = mybir.AxisListType

P = 128
T = 512
D = 1024
TB = T // P
DC = D // P
HD = 64
SSD_H, SSD_G, SSD_N, SSD_W = 8, 2, 128, 512
HPG = SSD_H // SSD_G
TAPS = 4
DIFF_H = 4
CHUNK = 64
XBC_C = 1024 // P
PH, NK, TOPK = 8, 128, 16
LISTS = 2 * PH
PAIRS = PH * TOPK
ROW_LEN = [TOPK // (i + 1) for i in range(TOPK)]
CAND = sum(ROW_LEN)
LONG_ROWS = sum(n > 1 for n in ROW_LEN)
PLE = 256
EPS = 1e-6
LAM_INIT = 0.2
NEG = -1e30
LOWEST = -3.0e38
MAGIC = 12582912.0

PI2_A = 6.28125
PI2_B = 2029.0 / 2**20
PI2_C = 2 * math.pi - PI2_A - PI2_B
INV_2PI = 1.0 / (2 * math.pi)

K_ID, K_TRI, K_NEG, K_IOTA, K_URO, K_NRO, K_INV = 0, 128, 256, 384, 512, 640, 704
K_END = 736
R_DTB, R_ALOG, R_DSK, R_QG, R_KG, R_LAM, R_DG, R_SG = 0, 8, 16, 24, 88, 152, 408, 536
R_END = 1048
C_MIX, C_FFN, C_GATE, C_CW, C_CB = 0, 8, 16, 24, 56
C_END = 64

UR = 4
GT = 32
STEP_TOK = 8
LOOP_A = 80
DT = T - P
U_RING = 3
DOTS_1, DOTS_T, DOTS_M, DOTS_J = 3, 15, 8, 12
V_RING = 4
GRP = 4


def reached(eng, sem, value):
    if not (isinstance(value, int) and value <= 0):
        eng.wait_ge(sem, value)


class Line:

    def __init__(self, eng, sem):
        self.eng, self.sem, self.count, self.last = eng, sem, {}, None

    def did(self, ins, sem=None):
        sem = sem or self.sem
        n = self.count[id(sem)] = self.count.get(id(sem), 0) + 1
        ins.then_inc(sem, 1)
        self.last = (sem, n)

    def settle(self):
        self.eng.wait_ge(*self.last)


def col(ap, i):
    return ap[:, i:i + 1]


def spread_last(ap, n):
    return ap.unsqueeze(len(ap.shape)).to_broadcast([*ap.shape, n])


class Semaphores:

    def __init__(self, nc):
        self.nc, self.all = nc, []

    def __call__(self, name):
        self.all.append(self.nc.alloc_semaphore(name))
        return self.all[-1]

    def free(self):
        self.nc.clear_and_free_semaphores(self.all)
        self.nc.all_engine_barrier()


class Weights:

    WIDTH = 256

    def __init__(self, sb, new_sem, tag, count):
        self.count = count
        self.raw = sb(f"{tag}_w_raw", [P, 2, DC, self.WIDTH])
        self.hi = sb(f"{tag}_w_hi", [P, 2, DC, self.WIDTH], F32R)
        self.lo = sb(f"{tag}_w_lo", [P, 2, DC, self.WIDTH], F32R)
        self.loaded, self.hi_ready, self.lo_ready, self.used = (
            [new_sem(f"{tag}_w_{n}{i}") for i in range(2)] for n in ("loaded", "hi_ready", "lo_ready", "used"))

    def load(self, sp, n, src):
        if n >= 2:
            sp.wait_ge(self.lo_ready[n % 2], n // 2)
        sp.dma_start(self.raw[:, n % 2, :, :], src.rearrange("p (c n) -> p c n", c=DC)).then_inc(self.loaded[n % 2], 16)

    def cut(self, pool):
        for n in range(self.count):
            s = n % 2
            pool.wait_ge(self.loaded[s], 16 * (n // 2 + 1))
            if n >= 2:
                pool.wait_ge(self.used[s], n // 2)
            pool.tensor_scalar(self.hi[:, s, :, :], self.raw[:, s, :, :], 1.0, 1.0, ALU.mult, ALU.mult).then_inc(self.hi_ready[s], 1)
            pool.wait_ge(self.hi_ready[s], n // 2 + 1)
            pool.tensor_tensor(self.lo[:, s, :, :], self.raw[:, s, :, :], self.hi[:, s, :, :].bitcast(F32), ALU.subtract)\
                .then_inc(self.lo_ready[s], 1)

    def ready(self, pe, n):
        pe.wait_ge(self.lo_ready[n % 2], n // 2 + 1)
        return self.hi[:, n % 2, :, :], self.lo[:, n % 2, :, :]


def product(pe, out, left, right):
    n_blocks = DC
    for d in range(n_blocks):
        pe.matmul(out, left(0, d), right(0, d), start=(d == 0), stop=False)
        pe.matmul(out, left(0, d), right(1, d), start=False, stop=False)
        last = pe.matmul(out, left(1, d), right(0, d), start=False, stop=(d == n_blocks - 1))
    return last


def mixer_tiles():
    out = []
    out += [(("xT", c), "turned_ready", c + 1) for c in range(DC)]
    out += [(("xbc", c), "conv_done", c + 1) for c in range(XBC_C)]
    out += [(("dt", 0), "dtraw_done", 1)]
    for n, (name, ready) in enumerate((("q", "qk_roped"), ("k", "qk_roped"), ("v", "v_ready"), ("z", "z_ready"))):
        base = 2 * TB if name == "k" else 0
        out += [((name, i), ready, base + i + 1) for i in range(2 * TB)]
    out += [(("qkT", i), "qkT_ready", i + 1) for i in range(2 * DIFF_H)]
    for t in range(TB):
        out += [(("xsT", t), "xs_ready", t + 1), (("bT", t), "btok_ready", t + 1)]
    for t in range(TB):
        out += [(("cs", t), "ncs_ready", t + 1)]
        out += [(("csb", t, g), "decay_ready", 2 * t + g + 1) for g in range(SSD_G)]
        out += [(("cb", t), "m_ready", 2 * t + 2)]
        out += [(("y", t), "y_ready", t + 1)]
        if t:
            out += [(("yo", t), "y_ready", t + 1)]
        if t < TB - 1:
            out += [(("st", t), "state_ready", t + 1)]
    units = TB * DIFF_H
    for i in range(units + 2):
        if i < units:
            out += [(("s", i, c), "probs_ready", 2 * i + c + 1) for c in range(2)]
        if 0 <= i - 1 < units:
            out += [(("aT", i - 1), "attnT_ready", i)]
        if 0 <= i - 2:
            out += [(("o", i - 2), "o_ready", i - 1)]
    out += [(("yT", c), "turned_ready", DC + c + 1) for c in range(DC)]
    out += [(("h", i), "h_ready", i + 1) for i in range(4 * TB)]
    return out


class Banks:

    def __init__(self, psum, tiles, sems, done):
        self.psum, self.sems, self.done = psum, sems, done
        self.index = {name: n for n, (name, _, _) in enumerate(tiles)}
        self.frees = [(s, v) for _, s, v in tiles]
        self.n = psum.shape[1]

    def at(self, *name):
        return self.psum[:, self.index[name] % self.n, :]

    def take(self, pe, *name):
        i = self.index[name] - self.n
        if i >= 0:
            s, v = self.frees[i]
            pe.wait_ge(self.sems[s], v)
        return self.at(*name)

    def filled(self, eng, *name):
        eng.wait_ge(self.done, self.index[name] + 1)
        return self.at(*name)


def mixer(nc, shared, io):
    h = shared["h"]
    con, cols = shared["con"], shared["cols"]
    N_IN = 12
    new_sem = Semaphores(nc)
    with ExitStack() as ctx:
        sb = lambda n, s, d=F32: ctx.enter_context(nc.sbuf_tensor(n, s, d))
        names = ["turned_ready", "nT_ready", "x_again", "wdt_hi_ready", "wdt_lo_ready", "conv_done", "dtraw_done", "qk_roped", "v_ready", "z_ready", "qkT_ready", "xs_ready",
                 "btok_ready", "ncs_ready", "decay_ready", "m_ready", "y_ready", "state_ready", "probs_ready",
                 "attnT_ready", "o_ready", "h_ready", "const_loaded", "x_loaded", "dtw_loaded", "pe_tile", "act_line",
                 "dve_line", "sumsq_ready", "ms_ready", "root_ready", "xn_ready", "sine_asked", "sine_ready",
                 "qksq_ready", "qkms_ready", "qkroot_ready", "qk_ready", "xbc_ready", "abs_ready", "edt_ready",
                 "dt_asked", "lam_asked", "lam_exp", "xdt_ready", "ecs_ready", "attn_ready", "bias_ready",
                 "fin_sq", "fin_ms", "fin_root", "mix_ready", "aexp_ready", "alog_go"]
        sem = {n: new_sem("m_" + n) for n in names}
        psum = ctx.enter_context(nc.psum_tensor("m_psum", [P, 8, 512], F32))
        bank = Banks(psum, mixer_tiles(), sem, sem["pe_tile"])

        weights = Weights(sb, new_sem, "m", N_IN + 4)
        wdt = sb("m_wdt", [P, DC, SSD_H])
        wdt_hi = sb("m_wdt_hi", [P, DC, SSD_H], F32R)
        wdt_lo = sb("m_wdt_lo", [P, DC, SSD_H], F32R)
        rows = sb("m_rows", [P, R_END])
        nT_hi = sb("m_nT_hi", [P, DC, T], F32R)
        nT_lo = sb("m_nT_lo", [P, DC, T], F32R)
        nT = (nT_hi, nT_lo)
        mix = h
        xbcT = sb("m_xbcT", [P, XBC_C, T])
        zs = sb("m_zs", [P, TB, SSD_W])
        v = sb("m_v", [P, TB, 512])
        qkT = sb("m_qkT", [P, 2 * DIFF_H, T])
        xs = sb("m_xs", [P, TB, SSD_W])
        btok = sb("m_btok", [P, TB, SSD_G * SSD_N])
        tab = sb("m_tab", [P, 4, TB, 2, HD // 2])
        ang = sb("m_ang", [P, 5, TB, HD // 2])
        x_in = xbcT[:, :, :].rearrange("p c t -> p (c t)").rearrange("p (t d) -> p t d", t=TB)
        posf = sb("m_posf", [P, TB])
        posi = sb("m_posi", [P, TB], I32)
        small = sb("m_small", [P, 64])
        ropeA = sb("m_ropeA", [P, 2, 512])
        ropeB = sb("m_ropeB", [P, 2, 512])
        qn = sb("m_qn", [P, TB, 2, 512])
        dts = sb("m_dts", [P, 8, TB, SSD_H])
        state = sb("m_state", [P, SSD_W])
        dec = sb("m_dec", [P, 2, HPG, P])
        ecl = sb("m_ecl", [P, SSD_H])
        Mt = tab[:, :, :, :, :].rearrange("p a t b c -> p (a t b c)").rearrange("p (h l) -> p h l", l=P)
        xdt = sb("m_xdt", [P, SSD_W])
        xdtd = sb("m_xdtd", [P, SSD_W])
        st8 = sb("m_st8", [P, 64])
        prob = qn[:, :, 1, :].rearrange("p (u c) n -> p u c n", u=2)
        attn = xbcT[:, 0:2, :]
        attnT = xbcT[:, 2:4, :].rearrange("p u (k q) -> p u k q", q=P)
        red = sb("m_red", [P, 8, 8])
        fin = sb("m_fin", [P, 4, 32])
        turned = ropeA
        sqj = dec[:, 0, :, :].rearrange("p a b -> p (a b)")

        ident = con[:, K_ID:K_ID + P]
        ss, ms, root, rstd = (small[:, 4 * i:4 * i + 4] for i in range(4))
        ssq, msq, rootq, rstdq = (fin[:, i, :] for i in range(4))
        qks = sb("m_qks", [P, 4, 4 * TB, 4])
        X_DT, X_NA, X_DA, X_NCS, X_ECS, X_A, X_B, X_C = range(8)
        a_rate = small[:, 16:24]
        lam = small[:, 24:30]
        qT = lambda hh: qkT[:, hh, :]
        kT = lambda hh: qkT[:, DIFF_H + hh, :]
        units = [(b, hh) for b in range(TB) for hh in range(DIFF_H)]

        block = ctx.enter_context(nc.Block())

        @block.sync
        def _(sp):
            sp.dma_start(con[:, :], io["consts"]).then_inc(sem["const_loaded"], 16)
            for t in range(TB):
                sp.dma_start(x_in[:, t, :], io["x"][t * P:(t + 1) * P, :]).then_inc(sem["x_loaded"], 16)
            sp.dma_start(cols[:, :], io["cols"]).then_inc(sem["const_loaded"], 16)
            sp.dma_start(rows[:, :], io["rows"]).then_inc(sem["const_loaded"], 16)
            sp.dma_start(posi[:, :], io["positions"]).then_inc(sem["const_loaded"], 16)
            sp.dma_start(wdt[:, :, :], io["w_dt"].rearrange("p (c n) -> p c n", c=DC)).then_inc(sem["dtw_loaded"], 16)
            for n in range(N_IN):
                weights.load(sp, n, io["w_in"][n])
            for n in range(4):
                weights.load(sp, N_IN + n, io["w_out"][n])
            sp.wait_ge(sem["pe_tile"], bank.index[("yT", DC - 1)] + 1)
            for t in range(TB):
                sp.dma_start(h[:, t, :], io["x"][t * P:(t + 1) * P, :]).then_inc(sem["x_again"], 16)

        @block.gpsimd
        def _(pool):
            pool.wait_ge(sem["dtw_loaded"], 16)
            pool.tensor_copy(wdt_hi[:, :, :], wdt[:, :, :]).then_inc(sem["wdt_hi_ready"], 1)
            pool.wait_ge(sem["wdt_hi_ready"], 1)
            pool.tensor_tensor(wdt_lo[:, :, :], wdt[:, :, :], wdt_hi[:, :, :].bitcast(F32), ALU.subtract).then_inc(sem["wdt_lo_ready"], 1)
            weights.cut(pool)

        @block.tensor
        def _(pe):
            def tile_done(ins):
                ins.then_inc(sem["pe_tile"], 1)

            pe.wait_ge(sem["const_loaded"], 64)
            pe.wait_ge(sem["xn_ready"], TB)
            for c in range(DC):
                out = bank.take(pe, "xT", c)
                for t in range(TB):
                    last = pe.transpose(out[:, t * P:(t + 1) * P], mix[:, t, c * P:(c + 1) * P], ident)
                tile_done(last)
            pe.wait_ge(sem["nT_ready"], DC)
            for c in range(XBC_C):
                w = weights.ready(pe, c // 2)
                out = bank.take(pe, "xbc", c)
                tile_done(product(pe, out, lambda part, d: w[part][:, d, (c % 2) * P:(c % 2 + 1) * P], lambda part, d: nT[part][:, d, :]))
                if c % 2:
                    pe.drain().then_inc(weights.used[c // 2 % 2], 1)
            pe.wait_ge(sem["wdt_lo_ready"], 1)
            out = bank.take(pe, "dt", 0)
            wd = (wdt_hi, wdt_lo)
            for t in range(TB):
                last = product(pe, out[:, t * 8:t * 8 + 8], lambda part, d: nT[part][:, d, t * P:(t + 1) * P], lambda part, d: wd[part][:, d, :])
            tile_done(last)
            for n in range(XBC_C // 2, N_IN):
                w = weights.ready(pe, n)
                name, half = "qkvz"[(n - 4) // 2], n % 2
                for t in range(TB):
                    out = bank.take(pe, name, half * TB + t)[:, 0:256]
                    tile_done(product(pe, out, lambda part, d: nT[part][:, d, t * P:(t + 1) * P], lambda part, d: w[part][:, d, :]))
                pe.drain().then_inc(weights.used[n % 2], 1)
            pe.wait_ge(sem["qk_ready"], 4 * TB)
            for i in range(2 * DIFF_H):
                out = bank.take(pe, "qkT", i)
                which, hh = i // DIFF_H, i % DIFF_H
                for t in range(TB):
                    last = pe.transpose(out[:, t * P:(t + 1) * P], qn[:, t, which, hh * P:(hh + 1) * P], ident)
                tile_done(last)
            pe.wait_ge(sem["xbc_ready"], XBC_C)
            for t in range(TB):
                out = bank.take(pe, "xsT", t)
                for c in range(4):
                    last = pe.transpose(out[:, c * P:(c + 1) * P], xbcT[:, c, t * P:(t + 1) * P], ident)
                tile_done(last)
                out = bank.take(pe, "bT", t)
                for c in range(SSD_G):
                    last = pe.transpose(out[:, c * P:(c + 1) * P], xbcT[:, 4 + c, t * P:(t + 1) * P], ident)
                tile_done(last)
            pe.wait_ge(sem["dt_asked"], 1)
            tri, neg = con[:, K_TRI:K_TRI + P], con[:, K_NEG:K_NEG + P]
            for t in range(TB):
                tok = slice(t * P, (t + 1) * P)
                out = bank.take(pe, "cs", t)
                tile_done(pe.matmul(out[:, 0:SSD_H], tri, dts[:, X_DA, t, :], start=True, stop=True))
                for g in range(SSD_G):
                    out = bank.take(pe, "csb", t, g)
                    for r in range(HPG):
                        da = dts[:, X_DA, t, g * HPG + r:g * HPG + r + 1]
                        pe.matmul(out[:, r * P:(r + 1) * P], da.to_broadcast([P, P]), tri, start=True, stop=False)
                        last = pe.matmul(out[:, r * P:(r + 1) * P], ident, neg, start=False, stop=True)
                    tile_done(last)
                out = bank.take(pe, "cb", t)
                for g in range(SSD_G):
                    last = pe.matmul(out[:, g * P:(g + 1) * P], xbcT[:, 4 + g, tok], xbcT[:, 6 + g, tok], start=True, stop=True)
                tile_done(last)
                pe.wait_ge(sem["xdt_ready"], 2 * t + 1)
                pe.wait_ge(sem["m_ready"], 2 * t + 2)
                out = bank.take(pe, "y", t)
                for hh in range(SSD_H):
                    last = pe.matmul(out[:, hh * HD:(hh + 1) * HD], Mt[:, hh, :], xdt[:, hh * HD:(hh + 1) * HD], start=True, stop=True)
                tile_done(last)
                if t:
                    pe.wait_ge(sem["state_ready"], t)
                    out = bank.take(pe, "yo", t)
                    for g in range(SSD_G):
                        last = pe.matmul(out[:, g * 256:(g + 1) * 256], xbcT[:, 6 + g, tok], state[:, g * 256:(g + 1) * 256], start=True, stop=True)
                    tile_done(last)
                if t < TB - 1:
                    pe.wait_ge(sem["btok_ready"], t + 1)
                    pe.wait_ge(sem["xdt_ready"], 2 * t + 2)
                    out = bank.take(pe, "st", t)
                    for g in range(SSD_G):
                        last = pe.matmul(out[:, g * 256:(g + 1) * 256], btok[:, t, g * P:(g + 1) * P], xdtd[:, g * 256:(g + 1) * 256], start=True, stop=True)
                    tile_done(last)
            pe.wait_ge(sem["qkT_ready"], 2 * DIFF_H)
            pe.wait_ge(sem["v_ready"], 2 * TB)
            for i in range(len(units) + 2):
                if i < len(units):
                    b, hh = units[i]
                    kend = (b + 1) * P
                    for c in range(2):
                        out = bank.take(pe, "s", i, c)
                        rowsl = slice(c * HD, (c + 1) * HD)
                        pe.matmul(out[:, 0:kend], qT(hh)[rowsl, b * P:kend], kT(hh)[rowsl, 0:kend], start=True, stop=False)
                        tile_done(pe.matmul(out[:, kend - CHUNK:kend], con[0:1, K_URO:K_URO + P], con[0:1, K_NRO:K_NRO + CHUNK],
                                            start=False, stop=True))
                if 0 <= i - 1 < len(units):
                    b, hh = units[i - 1]
                    pe.wait_ge(sem["attn_ready"], i)
                    out = bank.take(pe, "aT", i - 1)
                    for kb in range(b + 1):
                        last = pe.transpose(out[:, kb * P:(kb + 1) * P], attn[:, (i - 1) % 2, kb * P:(kb + 1) * P], ident)
                    tile_done(last)
                if 0 <= i - 2:
                    b, hh = units[i - 2]
                    pe.wait_ge(sem["attnT_ready"], i - 1)
                    out = bank.take(pe, "o", i - 2)
                    for kb in range(b + 1):
                        last = pe.matmul(out[:, 0:P], attnT[:, i % 2, kb, :], v[:, kb, hh * P:(hh + 1) * P], start=(kb == 0), stop=(kb == b))
                    tile_done(last)
            pe.wait_ge(sem["mix_ready"], 2 * TB)
            for c in range(DC):
                out = bank.take(pe, "yT", c)
                for t in range(TB):
                    last = pe.transpose(out[:, t * P:(t + 1) * P], mix[:, t, c * P:(c + 1) * P], ident)
                tile_done(last)
            pe.wait_ge(sem["nT_ready"], 2 * DC)
            for n in range(4):
                w = weights.ready(pe, N_IN + n)
                for t in range(TB):
                    out = bank.take(pe, "h", n * TB + t)[:, 0:256]
                    tile_done(product(pe, out, lambda part, d: nT[part][:, d, t * P:(t + 1) * P], lambda part, d: w[part][:, d, :]))
                pe.drain().then_inc(weights.used[n % 2], 1)

        @block.scalar
        def _(act):
            me = Line(act, sem["act_line"])
            act.wait_ge(sem["sine_asked"], 1)
            me.did(act.activation(ang[:, 3, :, :], ang[:, 0, :, :], ACT.Sin, scale=0.5), sem["sine_ready"])
            me.did(act.activation(ang[:, 4, :, :], ang[:, 0, :, :], ACT.Sin), sem["sine_ready"])
            for t in range(TB):
                act.wait_ge(sem["x_loaded"], 64)
                me.did(act.activation(mix[:, t, :], x_in[:, t, :], ACT.Square, accum_out=col(ss, t)), sem["sumsq_ready"])
            act.wait_ge(sem["ms_ready"], 1)
            me.did(act.activation(root, ms, ACT.Sqrt), sem["root_ready"])
            act.wait_ge(sem["const_loaded"], 64)
            for c in range(DC):
                src = bank.filled(act, "xT", c)
                if c >= 2:
                    act.wait_ge(sem["nT_ready"], c - 1)
                me.did(act.activation(turned[:, c % 2, :], src, ACT.Copy, scale=col(cols, C_MIX + c)), sem["turned_ready"])
            for i in range(4 * TB):
                src = bank.filled(act, "qk"[i // (2 * TB)], i % (2 * TB))[:, 0:256]
                if i:
                    act.wait_ge(sem["qkms_ready"], i)
                me.did(act.activation(sqj[:, 0:256], src, ACT.Square), sem["qksq_ready"])
                act.wait_ge(sem["qkms_ready"], i + 1)
                me.did(act.activation(qks[:, 1, i, :], qks[:, 0, i, :], ACT.Sqrt), sem["qkroot_ready"])
            for i in range(2 * TB):
                src = bank.filled(act, "v", i)[:, 0:256]
                half, t = i // TB, i % TB
                me.did(act.copy(v[:, t, half * 256:(half + 1) * 256], src), sem["v_ready"])
            for c in range(XBC_C):
                act.wait_ge(sem["conv_done"], c + 1)
                me.did(act.activation(xbcT[:, c, :], xbcT[:, c, :], ACT.Silu), sem["xbc_ready"])
            for i in range(2 * TB):
                src = bank.filled(act, "z", i)[:, 0:256]
                half, t = i // TB, i % TB
                me.did(act.activation(zs[:, t, half * 256:(half + 1) * 256], src, ACT.Silu), sem["z_ready"])
            for i in range(2 * DIFF_H):
                src = bank.filled(act, "qkT", i)
                me.did(act.copy(qkT[:, i, :], src), sem["qkT_ready"])
            act.wait_ge(sem["abs_ready"], 1)
            me.did(act.activation(dts[:, X_B, :, :], dts[:, X_A, :, :], ACT.Exp, scale=-1.0), sem["edt_ready"])
            me.did(act.activation(a_rate, rows[:, R_ALOG:R_ALOG + 8], ACT.Exp), sem["aexp_ready"])
            act.wait_ge(sem["lam_asked"], 1)
            me.did(act.activation(lam[:, 2:4], lam[:, 0:2], ACT.Exp), sem["lam_exp"])
            for t in range(TB):
                src = bank.filled(act, "xsT", t)
                me.did(act.copy(xs[:, t, :], src), sem["xs_ready"])
                src = bank.filled(act, "bT", t)
                me.did(act.copy(btok[:, t, :], src[:, 0:SSD_G * SSD_N]), sem["btok_ready"])
            for t in range(TB):
                act.wait_ge(sem["ncs_ready"], t + 1)
                me.did(act.activation(dts[:, X_ECS, t, :], dts[:, X_NCS, t, :], ACT.Exp, scale=-1.0), sem["ecs_ready"])
                for g in range(SSD_G):
                    src = bank.filled(act, "csb", t, g)
                    if t:
                        act.wait_ge(sem["m_ready"], 2 * t - 1 + g)
                        if t < TB:
                            act.wait_ge(sem["state_ready"], t)
                        act.wait_ge(sem["xdt_ready"], 2 * t)
                    for r in range(HPG):
                        hh = g * HPG + r
                        me.did(act.activation(dec[:, g, r, :], src[:, r * P:(r + 1) * P], ACT.Exp, bias=dts[:, X_NCS, t, hh:hh + 1]))
                    me.did(act.activation(ecl[:, g * HPG:(g + 1) * HPG], src.rearrange("p (r l) -> p r l", r=HPG)[:, :, P - 1], ACT.Exp),
                           sem["decay_ready"])
            for i in range(len(units) + 2):
                if i < len(units):
                    b, hh = units[i]
                    kend = (b + 1) * P
                    for c in range(2):
                        src = bank.filled(act, "s", i, c)
                        act.wait_ge(sem["bias_ready"], 2 * i + c + 1)
                        if i >= 2:
                            act.wait_ge(sem["attn_ready"], i - 1)
                        me.did(act.activation(prob[:, i % 2, c, 0:kend], src[:, 0:kend], ACT.Exp, bias=red[:, i % 8, 2 + c:3 + c],
                                              scale=HD ** -0.5, accum_out=red[:, i % 8, 4 + c:5 + c]), sem["probs_ready"])
                if 0 <= i - 1 < len(units):
                    b, hh = units[i - 1]
                    src = bank.filled(act, "aT", i - 1)
                    if i - 1 >= 2:
                        act.wait_ge(sem["pe_tile"], bank.index[("o", i - 3)] + 1)
                    me.did(act.copy(attnT[:, (i - 1) % 2, 0:b + 1, :], src[:, 0:(b + 1) * P].rearrange("p (k q) -> p k q", q=P)),
                           sem["attnT_ready"])
                if 0 <= i - 2:
                    b, hh = units[i - 2]
                    src = bank.filled(act, "o", i - 2)
                    me.did(act.copy(qn[:, b, 0, hh * P:(hh + 1) * P], src[:, 0:P]), sem["o_ready"])
            act.wait_ge(sem["fin_ms"], 1)
            me.did(act.activation(rootq[:, 0:24], msq[:, 0:24], ACT.Sqrt), sem["fin_root"])
            for c in range(DC):
                src = bank.filled(act, "yT", c)
                if c >= 2:
                    act.wait_ge(sem["nT_ready"], DC + c - 1)
                me.did(act.copy(turned[:, c % 2, :], src), sem["turned_ready"])

        @block.vector
        def _(dve):
            me = Line(dve, sem["dve_line"])

            def step(ins, s=None):
                me.did(ins, s)
                me.settle()

            dve.wait_ge(sem["const_loaded"], 64)
            step(dve.tensor_copy(posf[:, :], posi[:, :]))
            A0, A1, A2 = (ang[:, i, :, :] for i in range(3))
            inv = con[:, K_INV:K_INV + 32].unsqueeze(1).to_broadcast([P, TB, 32])
            step(dve.tensor_tensor(A0, inv, spread_last(posf[:, :], 32), ALU.mult))
            step(dve.tensor_scalar(A1, A0, INV_2PI, None, ALU.mult))
            step(dve.tensor_scalar(A2, A1, MAGIC, None, ALU.add))
            step(dve.tensor_scalar(A1, A2, MAGIC, None, ALU.subtract))
            for part in (PI2_A, PI2_B, PI2_C):
                step(dve.scalar_tensor_tensor(A0, A1, -part, A0, ALU.mult, ALU.add))
            step(dve.tensor_scalar(A0, A0, float(np.float32(3.1415925)), -float(np.float32(3.1415925)), ALU.min, ALU.max), sem["sine_asked"])
            dve.wait_ge(sem["sumsq_ready"], TB)
            step(dve.tensor_scalar(ms, ss, 1.0 / D, EPS, ALU.mult, ALU.add), sem["ms_ready"])
            dve.wait_ge(sem["root_ready"], 1)
            step(dve.reciprocal(rstd, root))
            for t in range(TB):
                me.did(dve.tensor_scalar(mix[:, t, :], x_in[:, t, :], col(rstd, t), None, ALU.mult), sem["xn_ready"])

            def two_parts(first):
                for c in range(DC):
                    dve.wait_ge(sem["turned_ready"], first + c + 1)
                    step(dve.tensor_copy(nT_hi[:, c, :], turned[:, c % 2, :]))
                    me.did(dve.tensor_tensor(nT_lo[:, c, :], turned[:, c % 2, :], nT_hi[:, c, :].bitcast(F32), ALU.subtract), sem["nT_ready"])

            two_parts(0)
            dve.wait_ge(sem["sine_ready"], 2)
            step(dve.tensor_tensor(A1, ang[:, 3, :, :], ang[:, 3, :, :], ALU.mult))
            step(dve.tensor_scalar(A1, A1, -2.0, 1.0, ALU.mult, ALU.add))
            for w, g0 in ((0, R_QG), (1, R_KG)):
                for half in range(2):
                    g_own = rows[:, g0 + 32 * half:g0 + 32 * half + 32].unsqueeze(1).to_broadcast([P, TB, 32])
                    g_other = rows[:, g0 + 32 * (1 - half):g0 + 32 * (1 - half) + 32].unsqueeze(1).to_broadcast([P, TB, 32])
                    me.did(dve.tensor_tensor(tab[:, 2 * w, :, half, :], A1, g_own, ALU.mult))
                    me.did(dve.scalar_tensor_tensor(tab[:, 2 * w + 1, :, half, :], ang[:, 4, :, :], 1.0 if half else -1.0, g_other,
                                                    ALU.mult, ALU.mult))
            for j in range(2):
                a0 = R_LAM + 128 * j
                me.did(dve.tensor_tensor_reduce(ropeA[:, 0, 64 * j:64 * j + 64], rows[:, a0:a0 + 64], rows[:, a0 + 64:a0 + 128], 1.0, 0.0,
                                                ALU.mult, ALU.add, col(lam, j)), None if j == 0 else sem["lam_asked"])
            me.settle()
            for c in range(XBC_C):
                src = bank.filled(dve, "xbc", c)
                tap = lambda k: col(cols, C_CW + TAPS * c + k)
                step(dve.tensor_scalar(xbcT[:, c, :], src, tap(3), col(cols, C_CB + c), ALU.mult, ALU.add))
                for k in (2, 1, 0):
                    s = 3 - k
                    step(dve.scalar_tensor_tensor(xbcT[:, c, s:T], src[:, 0:T - s], tap(k), xbcT[:, c, s:T], ALU.mult, ALU.add),
                         sem["conv_done"] if k == 0 else None)
            DT = lambda i: dts[:, i, :, :]
            src = bank.filled(dve, "dt", 0)
            bias = rows[:, R_DTB:R_DTB + 8].unsqueeze(1).to_broadcast([P, TB, 8])
            step(dve.tensor_tensor(DT(X_DT), src[:, 0:32].rearrange("p (t n) -> p t n", t=TB), bias, ALU.add), sem["dtraw_done"])
            step(dve.scalar_tensor_tensor(DT(X_A), DT(X_DT), -1.0, DT(X_DT), ALU.mult, ALU.max), sem["abs_ready"])
            for i in range(4 * TB):
                w, half, t = i // (2 * TB), i // TB % 2, i % TB
                src = bank.filled(dve, "qk"[w], half * TB + t)[:, 0:256]
                dve.wait_ge(sem["qksq_ready"], i + 1)
                step(dve.tensor_reduce(qks[:, 2, i, :], sqj[:, 0:256].rearrange("p (h d) -> p h d", d=HD), AX.X, ALU.add))
                me.did(dve.tensor_scalar(qks[:, 0, i, :], qks[:, 2, i, :], 1.0 / HD, EPS, ALU.mult, ALU.add), sem["qkms_ready"])
                two = lambda ap: ap.rearrange("p (h two r) -> p h two r", two=2, r=32)
                ra, rb = ropeA[:, i % 2, 0:256], ropeB[:, i % 2, 0:256]
                q4, a4, b4 = two(src), two(ra), two(rb)
                cosg = tab[:, 2 * w, t, :, :].unsqueeze(1).to_broadcast([P, 4, 2, 32])
                me.did(dve.tensor_tensor(a4, q4, cosg, ALU.mult))
                for side in range(2):
                    sing = tab[:, 2 * w + 1, t, side, :].unsqueeze(1).to_broadcast([P, 4, 32])
                    me.did(dve.tensor_tensor(b4[:, :, side, :], q4[:, :, 1 - side, :], sing, ALU.mult))
                me.settle()
                step(dve.tensor_tensor(ra, ra, rb, ALU.add), sem["qk_roped"])
                dve.wait_ge(sem["qkroot_ready"], i + 1)
                step(dve.reciprocal(qks[:, 3, i, :], qks[:, 1, i, :]))
                step(dve.tensor_tensor(qn[:, t, w, half * 256:(half + 1) * 256].rearrange("p (h d) -> p h d", d=HD),
                                       ra.rearrange("p (h d) -> p h d", d=HD), spread_last(qks[:, 3, i, :], HD), ALU.mult), sem["qk_ready"])
            dve.wait_ge(sem["edt_ready"], 1)
            step(dve.tensor_scalar(DT(X_A), DT(X_B), 2.0, None, ALU.add))
            step(dve.reciprocal(DT(X_C), DT(X_A)))
            step(dve.tensor_tensor(DT(X_A), DT(X_B), DT(X_C), ALU.mult))
            step(dve.tensor_tensor(DT(X_B), DT(X_A), DT(X_A), ALU.mult))
            step(dve.tensor_scalar(DT(X_C), DT(X_B), 2.0 / 17, 2.0 / 15, ALU.mult, ALU.add))
            for n in (13, 11, 9, 7, 5, 3, 1):
                step(dve.tensor_tensor(DT(X_C), DT(X_C), DT(X_B), ALU.mult))
                step(dve.tensor_scalar(DT(X_C), DT(X_C), 2.0 / n, None, ALU.add))
            step(dve.tensor_tensor(DT(X_C), DT(X_C), DT(X_A), ALU.mult))
            step(dve.scalar_tensor_tensor(DT(X_DT), DT(X_DT), 0.0, DT(X_C), ALU.max, ALU.add))
            dve.wait_ge(sem["aexp_ready"], 1)
            step(dve.scalar_tensor_tensor(DT(X_DA), DT(X_DT), -1.0, a_rate.unsqueeze(1).to_broadcast([P, TB, 8]), ALU.mult, ALU.mult),
                 sem["dt_asked"])
            dve.wait_ge(sem["lam_exp"], 1)
            step(dve.tensor_tensor(lam[:, 4:5], lam[:, 3:4], lam[:, 2:3], ALU.subtract))
            step(dve.tensor_scalar(lam[:, 5:6], lam[:, 4:5], LAM_INIT, None, ALU.subtract))
            h8 = lambda ap: ap.rearrange("p (h d) -> p h d", d=HD)
            for t in range(TB):
                src = bank.filled(dve, "cs", t)
                step(dve.tensor_scalar(dts[:, X_NCS, t, :], src[:, 0:SSD_H], -1.0, None, ALU.mult), sem["ncs_ready"])
                dve.wait_ge(sem["xs_ready"], t + 1)
                if t:
                    dve.wait_ge(sem["pe_tile"], bank.index[("st", t - 1)] + 1)
                step(dve.tensor_tensor(h8(xdt[:, :]), h8(xs[:, t, :]), spread_last(dts[:, X_DT, t, :], HD), ALU.mult), sem["xdt_ready"])
                dve.wait_ge(sem["decay_ready"], 2 * t + 2)
                dl = spread_last(dec[:, :, :, :].rearrange("p g r l -> p (g r) l")[:, :, P - 1], HD)
                me.did(dve.tensor_tensor(h8(xdtd[:, :]), h8(xdt[:, :]), dl, ALU.mult), sem["xdt_ready"])
                cb = bank.filled(dve, "cb", t)
                for g in range(SSD_G):
                    me.did(dve.tensor_tensor(Mt[:, g * HPG:(g + 1) * HPG, :], dec[:, g, :, :],
                                             cb[:, g * P:(g + 1) * P].unsqueeze(1).to_broadcast([P, HPG, P]), ALU.mult), sem["m_ready"])
                ym = mix[:, t, 0:SSD_W]
                if t == 0:
                    dve.wait_ge(sem["pe_tile"], bank.index[("xT", DC - 1)] + 1)
                step(dve.tensor_tensor(h8(ym), h8(xs[:, t, :]), spread_last(rows[:, R_DSK:R_DSK + 8], HD), ALU.mult))
                if t:
                    src = bank.filled(dve, "yo", t)
                    dve.wait_ge(sem["ecs_ready"], t + 1)
                    step(dve.tensor_tensor(h8(ropeA[:, 0, :]), h8(src), spread_last(dts[:, X_ECS, t, :], HD), ALU.mult))
                    step(dve.tensor_tensor(ym, ym, ropeA[:, 0, :], ALU.add))
                src = bank.filled(dve, "y", t)
                step(dve.tensor_tensor(ym, ym, src, ALU.add), sem["y_ready"])
                if t < TB - 1:
                    src = bank.filled(dve, "st", t)
                    if t == 0:
                        step(dve.tensor_copy(state[:, :], src), sem["state_ready"])
                    else:
                        step(dve.tensor_tensor(h8(state[:, :]), h8(state[:, :]), spread_last(ecl[:, :], HD), ALU.mult))
                        step(dve.tensor_tensor(state[:, :], state[:, :], src, ALU.add), sem["state_ready"])
                dve.wait_ge(sem["z_ready"], TB + t + 1)
                step(dve.tensor_tensor(ym, ym, zs[:, t, :], ALU.mult))
                for g in range(SSD_G):
                    yg = ym[:, g * 256:(g + 1) * 256]
                    me.did(dve.tensor_tensor_reduce(ropeB[:, 0, g * 256:(g + 1) * 256], yg, yg, 1.0, 0.0, ALU.mult, ALU.add, col(ssq, 2 * t + g)))
                me.settle()
            for i, (b, hh) in enumerate(units):
                kend = (b + 1) * P
                rd = red[:, i % 8, :]
                for c in range(2):
                    src = bank.filled(dve, "s", i, c)
                    step(dve.tensor_reduce(rd[:, c:c + 1], src[:, 0:kend], AX.X, ALU.max, negate=True))
                    step(dve.tensor_scalar(rd[:, 2 + c:3 + c], rd[:, c:c + 1], HD ** -0.5, None, ALU.mult), sem["bias_ready"])
                dve.wait_ge(sem["probs_ready"], 2 * i + 2)
                step(dve.reciprocal(rd[:, 6:8], rd[:, 4:6]))
                step(dve.tensor_tensor(rd[:, 7:8], rd[:, 7:8], lam[:, 5:6], ALU.mult))
                if i >= 2:
                    dve.wait_ge(sem["pe_tile"], bank.index[("aT", i - 2)] + 1)
                step(dve.tensor_scalar(attn[:, i % 2, 0:kend], prob[:, i % 2, 0, 0:kend], rd[:, 6:7], None, ALU.mult))
                step(dve.scalar_tensor_tensor(attn[:, i % 2, 0:kend], prob[:, i % 2, 1, 0:kend], rd[:, 7:8], attn[:, i % 2, 0:kend],
                                              ALU.mult, ALU.add), sem["attn_ready"])
            for b in range(TB):
                dve.wait_ge(sem["o_ready"], DIFF_H * (b + 1))
                for hh in range(DIFF_H):
                    o = qn[:, b, 0, hh * P:(hh + 1) * P]
                    me.did(dve.tensor_tensor_reduce(ropeA[:, b % 2, hh * P:(hh + 1) * P], o, o, 1.0, 0.0, ALU.mult, ALU.add,
                                                    col(ssq, 8 + 4 * b + hh)))
                me.settle()
            me.did(dve.tensor_scalar(msq[:, 0:8], ssq[:, 0:8], SSD_G / SSD_W, EPS, ALU.mult, ALU.add))
            step(dve.tensor_scalar(msq[:, 8:24], ssq[:, 8:24], 1.0 / P, EPS, ALU.mult, ALU.add), sem["fin_ms"])
            dve.wait_ge(sem["fin_root"], 1)
            step(dve.reciprocal(rstdq[:, 0:24], rootq[:, 0:24]))
            step(dve.tensor_scalar(rstdq[:, 8:24], rstdq[:, 8:24], 1.0 - LAM_INIT, None, ALU.mult))
            for t in range(TB):
                for g in range(SSD_G):
                    yg = mix[:, t, g * 256:(g + 1) * 256]
                    me.did(dve.scalar_tensor_tensor(yg, yg, col(rstdq, 2 * t + g), rows[:, R_SG + 256 * g:R_SG + 256 * g + 256], ALU.mult, ALU.mult),
                           sem["mix_ready"] if g else None)
                for hh in range(DIFF_H):
                    me.did(dve.scalar_tensor_tensor(mix[:, t, SSD_W + hh * P:SSD_W + (hh + 1) * P], qn[:, t, 0, hh * P:(hh + 1) * P],
                                                    col(rstdq, 8 + 4 * t + hh), rows[:, R_DG:R_DG + P], ALU.mult, ALU.mult),
                           sem["mix_ready"] if hh == DIFF_H - 1 else None)
            two_parts(DC)
            dve.wait_ge(sem["x_again"], 16 * TB)
            for n in range(4):
                for t in range(TB):
                    src = bank.filled(dve, "h", n * TB + t)[:, 0:256]
                    hv = h[:, t, n * 256:(n + 1) * 256]
                    me.did(dve.tensor_tensor(hv, hv, src, ALU.add), sem["h_ready"])
    new_sem.free()


def retrieval(nc, shared, io, h_dram):
    h, con, cols, hn_hi, hn_lo, scores = (shared[k] for k in ("h", "con", "cols", "hn_hi", "hn_lo", "scores"))
    new_sem = Semaphores(nc)
    with ExitStack() as ctx:
        sb = lambda n, s, d=F32: ctx.enter_context(nc.sbuf_tensor(n, s, d))
        names = ["sumsq_ready", "ms_ready", "root_ready", "xn_ready", "turned_ready", "nT_ready", "qT_ready", "scores_ready",
                 "k_loaded", "gain_loaded", "h_stored", "row_ready", "pe_tile", "act_line", "dve_line"]
        sem = {n: new_sem("r_" + n) for n in names}
        psum = ctx.enter_context(nc.psum_tensor("r_psum", [P, 8, 512], F32))
        tiles = [(("nT", c), "turned_ready", c + 1) for c in range(DC)]
        tiles += [(("q", f), "qT_ready", f + 1) for f in range(LISTS)]
        tiles += [(("s", i), "scores_ready", i + 1) for i in range(TB * LISTS // 4)]
        bank = Banks(psum, tiles, sem, sem["pe_tile"])
        weights = Weights(sb, new_sem, "r", LISTS // 2)
        keys = sb("r_keys", [P, 2, NK])
        qx = sb("r_qx", [P, LISTS, T])
        turned = sb("r_turned", [P, 2, T])
        gain = sb("r_gain", [P, D])
        hn = (hn_hi, hn_lo)
        small = sb("r_small", [P, 16])
        ss, ms, root, rstd = (small[:, 4 * i:4 * i + 4] for i in range(4))
        ident = con[:, K_ID:K_ID + P]
        xn = lambda t: qx[:, 2 * t:2 * t + 2, :].rearrange("p a n -> p (a n)")
        block = ctx.enter_context(nc.Block())

        @block.sync
        def _(sp):
            sp.dma_start(keys[:, :, :], io["keys"].rearrange("p (a k) -> p a k", a=2)).then_inc(sem["k_loaded"], 16)
            sp.dma_start(gain[:, :], io["ffn_gain"]).then_inc(sem["gain_loaded"], 16)
            for t in range(TB):
                sp.dma_start(h_dram[t], h[:, t, :]).then_inc(sem["h_stored"], 16)
            for n in range(LISTS // 2):
                weights.load(sp, n, io["w_q"][n])
            sp.wait_ge(sem["h_stored"], 16 * TB)

        @block.gpsimd
        def _(pool):
            weights.cut(pool)

        @block.tensor
        def _(pe):
            pe.wait_ge(sem["xn_ready"], TB)
            for c in range(DC):
                out = bank.take(pe, "nT", c)
                for t in range(TB):
                    last = pe.transpose(out[:, t * P:(t + 1) * P], xn(t)[:, c * P:(c + 1) * P], ident)
                last.then_inc(sem["pe_tile"], 1)
            pe.wait_ge(sem["nT_ready"], DC)
            for f in range(LISTS):
                w = weights.ready(pe, f // 2)
                out = bank.take(pe, "q", f)
                last = product(pe, out, lambda part, d: w[part][:, d, (f % 2) * P:(f % 2 + 1) * P], lambda part, d: hn[part][:, d, :])
                last.then_inc(sem["pe_tile"], 1)
                if f % 2:
                    pe.drain().then_inc(weights.used[f // 2 % 2], 1)
            pe.wait_ge(sem["k_loaded"], 16)
            pe.wait_ge(sem["qT_ready"], LISTS)
            for i in range(TB * LISTS // 4):
                t, f0 = i // 4, (i % 4) * 4
                out = bank.take(pe, "s", i)
                for j in range(4):
                    last = pe.matmul(out[:, j * NK:(j + 1) * NK], qx[:, f0 + j, t * P:(t + 1) * P], keys[:, j % 2, :], start=True, stop=True)
                last.then_inc(sem["pe_tile"], 1)

        @block.scalar
        def _(act):
            me = Line(act, sem["act_line"])
            for t in range(TB):
                me.did(act.activation(xn(t), h[:, t, :], ACT.Square, accum_out=col(ss, t)), sem["sumsq_ready"])
            act.wait_ge(sem["ms_ready"], 1)
            me.did(act.activation(root, ms, ACT.Sqrt), sem["root_ready"])
            for c in range(DC):
                src = bank.filled(act, "nT", c)
                if c >= 2:
                    act.wait_ge(sem["nT_ready"], c - 1)
                me.did(act.activation(turned[:, c % 2, :], src, ACT.Copy, scale=col(cols, C_FFN + c)), sem["turned_ready"])
            act.wait_ge(sem["row_ready"], 1)
            for f in range(LISTS):
                src = bank.filled(act, "q", f)
                me.did(act.copy(qx[:, f, :], src), sem["qT_ready"])

        @block.vector
        def _(dve):
            me = Line(dve, sem["dve_line"])
            dve.wait_ge(sem["sumsq_ready"], TB)
            me.did(dve.tensor_scalar(ms, ss, 1.0 / D, EPS, ALU.mult, ALU.add), sem["ms_ready"])
            dve.wait_ge(sem["root_ready"], 1)
            me.did(dve.reciprocal(rstd, root))
            me.settle()
            for t in range(TB):
                me.did(dve.tensor_scalar(xn(t), h[:, t, :], col(rstd, t), None, ALU.mult), sem["xn_ready"])
            dve.wait_ge(sem["gain_loaded"], 16)
            dve.wait_ge(sem["h_stored"], 16 * TB)
            me.settle()
            me.did(dve.tensor_tensor(h[:, TB - 1, :], xn(0), gain[:, :], ALU.mult), sem["row_ready"])
            for c in range(DC):
                dve.wait_ge(sem["turned_ready"], c + 1)
                me.did(dve.tensor_copy(hn_hi[:, c, :], turned[:, c % 2, :]))
                me.settle()
                me.did(dve.tensor_tensor(hn_lo[:, c, :], turned[:, c % 2, :], hn_hi[:, c, :].bitcast(F32), ALU.subtract), sem["nT_ready"])
            for i in range(TB * LISTS // 4):
                src = bank.filled(dve, "s", i)
                me.did(dve.tensor_copy(scores[:, i // 4, (i % 4) * 4:(i % 4) * 4 + 4, :], src.rearrange("p (l k) -> p l k", k=NK)),
                       sem["scores_ready"])
    new_sem.free()


def scoring(nc, shared, io, act_dram, gate_dram):
    con, hn_hi, hn_lo, scores, h, w0, v_row = (shared[k] for k in ("con", "hn_hi", "hn_lo", "scores", "h", "w0", "v_row"))
    rows, hn_row = h[:, 0:U_RING, :], h[:, TB - 1, :]
    WAITS = 25
    OPS = 1 + 5 * LISTS + 2 + 2 * (LONG_ROWS + 1) + 5 * PH + 2 + 6 + 4 + WAITS
    n_steps = NK
    new_sem = Semaphores(nc)
    with ExitStack() as ctx:
        sb = lambda n, s, d=F32: ctx.enter_context(nc.sbuf_tensor(n, s, d))
        S = lambda n: new_sem("s_" + n)
        ring = lambda n, k: [S(f"{n}{i}") for i in range(k)]
        u_loaded, hi_ready, lo_ready, u_scored, act_ready, act_stored = (
            ring(n, UR) for n in ("u_loaded", "hi_ready", "lo_ready", "u_scored", "act_ready", "act_stored"))
        spread_ready, gates_summed, gates_copied = (ring(n, 2) for n in ("spread_ready", "gates_summed", "gates_copied"))
        tile_stored = ring("tile_stored", 2)
        row_loaded, dotted = ring("row_loaded", U_RING), ring("dotted", U_RING)
        rows_known, dots_ready, w0_gelu = S("rows_known"), S("dots_ready"), S("w0_gelu")
        dve_line, act_line = S("dve_line"), S("act_line")
        exp_ready, found_ready, turned, turned_copied = (
            S(n) for n in ("exp_ready", "found_ready", "turned", "turned_copied"))
        psU = ctx.enter_context(nc.psum_tensor("s_psU", [P, UR, 512], F32))
        psG = ctx.enter_context(nc.psum_tensor("s_psG", [P, 2, 2, 4, P], F32))

        u_raw = sb("s_u_raw", [P, UR, DC * P])
        u_hi = sb("s_u_hi", [P, UR, DC * P], F32R)
        u_lo = sb("s_u_lo", [P, UR, DC * P], F32R)
        acts = sb("s_acts", [P, UR, DT])
        pair = sb("s_pair", [P, 3, DT])
        onehot = sb("s_onehot", [P, 2, 2, STEP_TOK, P])
        gtile = sb("s_gtile", [P, 2, NK, GT])
        work = gtile[:, :, :, :].rearrange("p a i t -> p a (i t)")
        match = work[:, 0, 0:4 * TOPK * CAND].rearrange("p (h k c) -> p h k c", h=4, k=TOPK)
        cut = {}
        at = 0
        for name, n in (("s_cur", LISTS * NK), ("best", LISTS * TOPK), ("bestf", LISTS * TOPK), ("cand", 2 * PH * CAND), ("cid", PH * CAND)):
            cut[name] = work[:, 1, at:at + n]
            at += n
        assert at <= NK * GT and 4 * TOPK * CAND <= NK * GT
        s_cur = cut["s_cur"].rearrange("p (l k) -> p l k", l=LISTS)
        best, bestf = (cut[n].rearrange("p (l k) -> p l k", l=LISTS) for n in ("best", "bestf"))
        cand = cut["cand"].rearrange("p (a h c) -> p a h c", a=2, h=PH)
        cid = cut["cid"].rearrange("p (h c) -> p h c", h=PH)
        hold = sb("s_hold", [P, 1])
        u_row = sb("s_u_row", [P, PAIRS], U32)
        dots = sb("s_dots", [P, PAIRS])
        dot_slot = sb("s_dot_slot", [P, 16])
        besti = sb("s_besti", [P, LISTS, TOPK], U32)
        top = sb("s_top", [P, PH, TOPK])
        pos = sb("s_pos", [P, PH, TOPK], U32)
        posf = sb("s_posf", [P, PH, TOPK])
        idi = sb("s_idi", [P, 3, PAIRS], I32)
        found = sb("s_found", [P, TB, 3, PAIRS])
        zsum = sb("s_zsum", [P, 2, TB * PH])
        ident, iota = con[:, K_ID:K_ID + P], con[:, K_IOTA:K_IOTA + P]

        block = ctx.enter_context(nc.Block())

        @block.sync
        def _(sp):
            def load(step, s):
                sp.dma_start(u_raw[:, s, :], io["u_t"][step]).then_inc(u_loaded[s], 16)

            for s in range(UR):
                load(s, s)
            with sp.Fori(1, n_steps // UR) as it:
                for s in range(UR):
                    sp.wait_ge(lo_ready[s], it)
                    load(it * UR + s, s)
                    sp.wait_ge(act_ready[s], it)
                    sp.dma_start(act_dram[it * UR + (s - UR)], acts[:, s, :]).then_inc(act_stored[s], 16)
            for s in range(UR):
                sp.wait_ge(act_ready[s], n_steps // UR)
                sp.dma_start(act_dram[n_steps - UR + s], acts[:, s, :]).then_inc(act_stored[s], 16)
            for s in range(UR):
                sp.wait_ge(act_stored[s], 16 * (n_steps // UR))

        @block.gpsimd
        def _(pool):
            pair_no = 0

            def gather():
                nonlocal pair_no
                c, s = pair_no, pair_no % U_RING
                if c == 0:
                    pool.wait_ge(rows_known, 1)
                reached(pool, dotted[s], c // U_RING)
                pool.indirect_dma_start(rows[:, s, :], None, io["u_rows"], bass.IndirectOffsetOnAxis(ap=u_row[:, c:c + 1], axis=0),
                                        bounds_check=NK * NK - 1).then_inc(row_loaded[s], 16)
                pair_no += 1

            for n in range(n_steps):
                s, it = n % UR, n // UR
                pool.wait_ge(hi_ready[s], it + 1)
                reached(pool, u_scored[s], it)
                pool.tensor_tensor(u_lo[:, s, :], u_raw[:, s, :], u_hi[:, s, :].bitcast(F32), ALU.subtract).then_inc(lo_ready[s], 1)
                if LOOP_A // 5 <= n < LOOP_A and n % 4 != 3:
                    gather()
                if n == LOOP_A - 1:
                    for _ in range(DOTS_M):
                        gather()
                if n >= LOOP_A:
                    for _ in range(2 - n % 2):
                        gather()
            assert pair_no == PAIRS

        @block.tensor
        def _(pe):
            def score(it, s):
                pe.wait_ge(lo_ready[s], it + 1)
                reached(pe, act_ready[s], it)
                for d in range(DC):
                    for n, (uu, hh) in enumerate(((u_hi, hn_hi), (u_hi, hn_lo), (u_lo, hn_hi))):
                        last = pe.matmul(psU[:, s, 0:DT], uu[:, s, d * P:(d + 1) * P], hh[:, d, P:T],
                                         start=(n == 0 and d == 0), stop=(n == 2 and d == DC - 1))
                last.then_inc(u_scored[s], 1)

            for s in range(UR):
                score(0, s)
            with pe.Fori(1, LOOP_A // UR) as it:
                for s in range(UR):
                    score(it, s)
            pe.wait_ge(found_ready, 1)
            for j in range(3):
                for t in range(1, TB):
                    last = pe.transpose(psG[:, j // 2, j % 2, t - 1, :], found[:, t, j, :], ident)
            last.then_inc(turned, 1)

            def spread_and_score(j):
                for k in range(8):
                    par = k % 2
                    pe.wait_ge(spread_ready[par], 4 * j + k // 2 + 1)
                    reached(pe, gates_copied[par], 4 * j + k // 2)
                    for n in range(STEP_TOK):
                        last = pe.matmul(psG[:, par, n // 4, n % 4, :], onehot[:, par, 0, n, :], onehot[:, par, 1, n, :],
                                         start=True, stop=True)
                    last.then_inc(gates_summed[par], 1)
                    score(2 * j + (LOOP_A // UR + k // UR), k % UR)

            spread_and_score(0)
            with pe.Fori(1, (n_steps - LOOP_A) // 8) as j:
                spread_and_score(j)

        @block.scalar
        def _(act):
            def split(it, s):
                act.wait_ge(u_loaded[s], 16 * it + 16)
                reached(act, u_scored[s], it)
                reached(act, lo_ready[s], it)
                act.copy(u_hi[:, s, :], u_raw[:, s, :]).then_inc(hi_ready[s], 1)

            def gelu(it, s):
                act.wait_ge(u_scored[s], it + 1)
                reached(act, act_stored[s], 16 * it)
                act.activation(acts[:, s, :], psU[:, s, 0:DT], ACT.Gelu).then_inc(act_ready[s], 1)

            split(0, 0)
            split(0, 1)
            for s in range(UR):
                split((s + 2) // UR, (s + 2) % UR)
                gelu(0, s)
            with act.Fori(1, LOOP_A // UR) as it:
                for s in range(UR):
                    split(it + (s + 2) // UR, (s + 2) % UR)
                    gelu(it, s)
            act.wait_ge(dve_line, TB * OPS)
            act.activation(found[:, :, 2, :], found[:, :, 2, :], ACT.Exp).then_inc(exp_ready, 1)
            last = n_steps - LOOP_A
            n_it = last // 8

            def steps(j, final):
                for k in range(8):
                    par, tile = k % 2, k // 4
                    if not (final and k >= 6):
                        split(2 * j + (LOOP_A // UR + (k + 2) // UR), (k + 2) % UR)
                    act.wait_ge(gates_summed[par], 4 * j + k // 2 + 1)
                    if k % 4 == 0:
                        reached(act, tile_stored[tile], 16 * j)
                    for half in range(2):
                        t0 = (k % 4) * STEP_TOK + half * 4
                        ins = act.copy(gtile[:, tile, :, t0:t0 + 4].rearrange("p i t -> p t i"), psG[:, par, half, :, :])
                        ins.then_inc(gates_copied[par] if half else act_line, 1)
                    gelu(2 * j + (LOOP_A // UR + k // UR), k % UR)
                    if k % 4 == 3:
                        act.wait_ge(gates_copied[1], 4 * j + k // 2 + 1)
                        act.dma_start(gate_dram[2 * j + tile], gtile[:, tile, :, :]).then_inc(tile_stored[tile], 16)

            steps(0, False)
            with act.Fori(1, n_it - 1) as j:
                steps(j, False)
            steps(n_it - 1, True)
            act.wait_ge(dots_ready, 1)
            act.activation(w0[:, :], dots[:, :], ACT.Gelu).then_inc(w0_gelu, 1)
            for tile in range(2):
                act.wait_ge(tile_stored[tile], 16 * n_it)

        @block.vector
        def _(dve):
            def dot(s, rounds, k):
                dve.wait_ge(row_loaded[s], 16 * rounds)
                dve.tensor_tensor_reduce(rows[:, s, :], rows[:, s, :], hn_row, 1.0, 0.0, ALU.mult, ALU.add, col(dot_slot, k))\
                    .then_inc(dotted[s], 1)

            def retrieve(t, n_dots):
                me = Line(dve, dve_line)
                did = me.did
                n_waits = 0

                def wait():
                    nonlocal n_waits
                    if 1 <= n_waits <= n_dots:
                        k = n_waits - 1
                        dot((DOTS_1 + k) % U_RING, DOTS_T // U_RING * (t - 1) + (DOTS_1 + k) // U_RING + 1, k)
                    n_waits += 1
                    dve.wait_ge(dve_line, me.count[id(dve_line)] + t * OPS)
                    did(dve.memset(hold[:, :], 0.0))

                did(dve.tensor_copy(s_cur[:, :, :], scores[:, t, :, :]))
                wait()
                for l in range(LISTS):
                    did(dve.max(best[:, l, 0:8], s_cur[:, l, :]))
                wait()
                for l in range(LISTS):
                    did(dve.max_index(besti[:, l, 0:8], best[:, l, 0:8], s_cur[:, l, :]))
                wait()
                for l in range(LISTS):
                    did(dve.match_replace(s_cur[:, l, :], best[:, l, 0:8], s_cur[:, l, :], LOWEST))
                wait()
                for l in range(LISTS):
                    did(dve.max(best[:, l, 8:16], s_cur[:, l, :]))
                wait()
                for l in range(LISTS):
                    did(dve.max_index(besti[:, l, 8:16], best[:, l, 8:16], s_cur[:, l, :]))
                wait()
                did(dve.tensor_copy(bestf[:, :, :], besti[:, :, :]))
                wait()
                b4 = best[:, :, :].rearrange("p (h two) k -> p h two k", two=2)
                i4 = bestf[:, :, :].rearrange("p (h two) k -> p h two k", two=2)
                did(dve.tensor_scalar(i4[:, :, 0, :], i4[:, :, 0, :], float(NK), None, ALU.mult))
                wait()
                for out, src in ((cand[:, 0, :, :], b4), (cid, i4)):
                    at = 0
                    for i in range(LONG_ROWS):
                        n = ROW_LEN[i]
                        did(dve.tensor_tensor(out[:, :, at:at + n], src[:, :, 1, 0:n], src[:, :, 0, i:i + 1].to_broadcast([P, PH, n]), ALU.add))
                        at += n
                    did(dve.tensor_tensor(out[:, :, at:CAND], src[:, :, 0, LONG_ROWS:TOPK],
                                          src[:, :, 1, 0:1].to_broadcast([P, PH, TOPK - LONG_ROWS]), ALU.add))
                wait()
                for hh in range(PH):
                    did(dve.max(top[:, hh, 0:8], cand[:, 0, hh, :]))
                wait()
                for hh in range(PH):
                    did(dve.max_index(pos[:, hh, 0:8], top[:, hh, 0:8], cand[:, 0, hh, :]))
                for hh in range(PH):
                    did(dve.match_replace(cand[:, 1, hh, :], top[:, hh, 0:8], cand[:, 0, hh, :], LOWEST))
                wait()
                for hh in range(PH):
                    did(dve.max(top[:, hh, 8:16], cand[:, 1, hh, :]))
                wait()
                for hh in range(PH):
                    did(dve.max_index(pos[:, hh, 8:16], top[:, hh, 8:16], cand[:, 1, hh, :]))
                wait()
                did(dve.tensor_copy(posf[:, :, :], pos[:, :, :]))
                did(dve.tensor_tensor(found[:, t, 2, :].rearrange("p (h k) -> p h k", h=PH), top[:, :, :],
                                      top[:, :, 0:1].to_broadcast([P, PH, TOPK]), ALU.subtract))
                wait()
                for half in range(2):
                    hs = slice(4 * half, 4 * half + 4)
                    io50 = iota[:, 0:CAND].unsqueeze(1).unsqueeze(1).to_broadcast([P, 4, TOPK, CAND])
                    did(dve.tensor_tensor(match, io50, spread_last(posf[:, hs, :], CAND), ALU.is_equal))
                    wait()
                    did(dve.tensor_tensor(match, match, cid[:, hs, :].unsqueeze(2).to_broadcast([P, 4, TOPK, CAND]), ALU.mult))
                    wait()
                    did(dve.tensor_reduce(posf[:, hs, :], match, AX.X, ALU.add))
                    wait()
                did(dve.tensor_copy(idi[:, 0, :], posf[:, :, :].rearrange("p h k -> p (h k)")))
                wait()
                did(dve.tensor_scalar(idi[:, 1, :], idi[:, 0, :], 7, None, ALU.arith_shift_right))
                did(dve.tensor_scalar(idi[:, 2, :], idi[:, 0, :], NK - 1, None, ALU.bitwise_and))
                wait()
                did(dve.tensor_copy(found[:, t, 0:2, :], idi[:, 1:3, :]))
                wait()
                if n_dots:
                    dve.wait_ge(dotted[(DOTS_1 + n_dots - 1) % U_RING], DOTS_T // U_RING * (t - 1) + (DOTS_1 + n_dots - 1) // U_RING + 1)
                    did(dve.tensor_copy(dots[:, bass.ds(t * DOTS_T + (DOTS_1 - DOTS_T), DOTS_T)], dot_slot[:, 0:DOTS_T]))
                else:
                    did(dve.memset(dots[:, :], 0.0))
                wait()
                assert me.count[id(dve_line)] == OPS, me.count[id(dve_line)]

            retrieve(0, 0)
            dve.tensor_copy(u_row[:, :], idi[:, 0, :]).then_inc(rows_known, 1)
            dve.scalar_tensor_tensor(v_row[:, :], found[:, 0, 1, :], float(NK), found[:, 0, 0, :], ALU.mult, ALU.add).then_inc(rows_known, 1)
            dve.wait_ge(rows_known, 2)
            for k in range(DOTS_1):
                dot(k % U_RING, 1, k)
            dve.wait_ge(dotted[(DOTS_1 - 1) % U_RING], 1)
            dve.tensor_copy(dots[:, 0:DOTS_1], dot_slot[:, 0:DOTS_1]).then_inc(rows_known, 1)
            dve.wait_ge(rows_known, 3)
            with dve.Fori(1, TB) as t:
                retrieve(t, DOTS_T)
            done = TB * OPS
            for k in range(DOTS_M):
                c = DOTS_1 + (TB - 1) * DOTS_T + k
                dot(c % U_RING, c // U_RING + 1, k)

            def step(ins):
                nonlocal done
                ins.then_inc(dve_line, 1)
                done += 1
                dve.wait_ge(dve_line, done)

            c0 = DOTS_1 + (TB - 1) * DOTS_T
            dve.wait_ge(dotted[(c0 + DOTS_M - 1) % U_RING], (c0 + DOTS_M - 1) // U_RING + 1)
            step(dve.tensor_copy(dots[:, c0:c0 + DOTS_M], dot_slot[:, 0:DOTS_M]))
            c0 += DOTS_M
            dve.wait_ge(exp_ready, 1)
            e3 = found[:, :, 2, :].rearrange("p t (h k) -> p t h k", h=PH)
            z2 = zsum[:, :, :].rearrange("p a (t h) -> p a t h", t=TB)
            step(dve.tensor_reduce(z2[:, 0, :, :], e3, AX.X, ALU.add))
            step(dve.reciprocal(zsum[:, 1, :], zsum[:, 0, :]))
            dve.tensor_tensor(e3, e3, spread_last(z2[:, 1, :, :], TOPK), ALU.mult).then_inc(found_ready, 1)
            dve.wait_ge(turned, 1)
            for j in range(3):
                ins = dve.tensor_copy(pair[:, j, :], psG[:, j // 2, j % 2, 0:TB - 1, :].rearrange("p a b -> p (a b)"))
                ins.then_inc(turned_copied, 1)
            dve.wait_ge(turned_copied, 3)
            iota3 = iota.unsqueeze(1).to_broadcast([P, STEP_TOK, P])

            def spread(j):
                n = 0
                for k in range(8):
                    par = k % 2
                    tok = lambda a: spread_last(pair[:, a, bass.ds(j * (8 * STEP_TOK) + k * STEP_TOK, STEP_TOK)], P)
                    reached(dve, gates_summed[par], 4 * j + k // 2)
                    first = dve.tensor_tensor(onehot[:, par, 0, :, :], iota3, tok(0), ALU.is_equal)
                    first.then_inc(dve_line, 1)
                    dve.wait_ge(dve_line, 17 * j + (done + 2 * k + 1))
                    dve.tensor_tensor(onehot[:, par, 0, :, :], onehot[:, par, 0, :, :], tok(2), ALU.mult).then_inc(dve_line, 1)
                    dve.tensor_tensor(onehot[:, par, 1, :, :], iota3, tok(1), ALU.is_equal).then_inc(spread_ready[par], 1)
                    for _ in range(2 - par):
                        c = c0 + n
                        dot(c % U_RING, DOTS_J // U_RING * j + c // U_RING + 1, n)
                        n += 1
                dve.wait_ge(dotted[c % U_RING], DOTS_J // U_RING * j + c // U_RING + 1)
                dve.tensor_copy(dots[:, bass.ds(j * DOTS_J + c0, DOTS_J)] if not isinstance(j, int) else dots[:, j * DOTS_J + c0:(j + 1) * DOTS_J + c0],
                                dot_slot[:, 0:DOTS_J]).then_inc(dve_line, 1)

            spread(0)
            with dve.Fori(1, (n_steps - LOOP_A) // 8) as j:
                spread(j)
            n_j = (n_steps - LOOP_A) // 8
            assert c0 + n_j * DOTS_J == PAIRS
            done += 17 * n_j
            dve.wait_ge(dve_line, done)
            dve.memset(hold[:, :], 0.0).then_inc(dots_ready, 1)
            dve.wait_ge(w0_gelu, 1)
            step(dve.tensor_tensor(w0[:, :], w0[:, :], found[:, 0, 2, :], ALU.mult))
    new_sem.free()


def values(nc, shared, io, act_dram, gate_dram, h_dram):
    h, w0, v_row = (shared[k] for k in ("h", "w0", "v_row"))
    n_grp = NK // GRP
    OUTS = 2 * (TB - 1)
    new_sem = Semaphores(nc)
    with ExitStack() as ctx:
        sb = lambda n, s, d=F32: ctx.enter_context(nc.sbuf_tensor(n, s, d))
        S = lambda n: new_sem("v_" + n)
        ring = lambda n, k: [S(f"{n}{i}") for i in range(k)]
        v_loaded, vhi_ready, vlo_ready = (ring(n, GRP) for n in ("v_loaded", "vhi_ready", "vlo_ready"))
        in_loaded, wg_ready, whi_ready, wlo_ready = (ring(n, 2) for n in ("in_loaded", "wg_ready", "whi_ready", "wlo_ready"))
        out_ready = [ring(f"out_ready{par}_", OUTS) for par in range(2)]
        out_added = ring("out_added", OUTS)
        row_loaded, row_added = ring("row_loaded", V_RING), ring("row_added", V_RING)
        h_loaded = S("h_loaded")
        group_done = [out_ready[par][OUTS - 1] for par in range(2)]
        ps = ctx.enter_context(nc.psum_tensor("v_ps", [P, OUTS, 512], F32))
        v_raw = sb("v_raw", [P, GRP, D])
        v_hi = sb("v_hi", [P, 2, GRP, D], F32R)
        v_lo = sb("v_lo", [P, 2, GRP, D], F32R)
        a_in = sb("v_act", [P, 2, GRP, DT])
        g_in = sb("v_gate", [P, 2, DT // GT, GRP, GT])
        w_hi = sb("v_whi", [P, 2, GRP, DT], F32R)
        w_lo = sb("v_wlo", [P, 2, GRP, DT], F32R)
        rows = sb("v_rows", [P, V_RING, D])
        v_rows = io["v_t"].rearrange("i p d -> (i p) d")
        assert n_grp * V_RING == PAIRS
        block = ctx.enter_context(nc.Block())

        @block.sync
        def _(sp):
            def group(g, it, par, first):
                if not first:
                    sp.wait_ge(wlo_ready[par], it)
                sp.dma_start(a_in[:, par, :, :], act_dram[bass.ds(g * GRP, GRP)].rearrange("i p t -> p i t")).then_inc(in_loaded[par], 16)
                sp.dma_start(g_in[:, par, :, :, :], gate_dram[:, :, bass.ds(g * GRP, GRP), :].rearrange("g p i t -> p g i t")).then_inc(in_loaded[par], 16)
                for n in range(GRP):
                    if not (first and par == 0):
                        sp.wait_ge(vlo_ready[n], 2 * it + par)
                    sp.dma_start(v_raw[:, n, :], io["v_t"][g * GRP + n]).then_inc(v_loaded[n], 16)

            for t in range(TB):
                sp.dma_start(h[:, t, :], h_dram[t]).then_inc(h_loaded, 16)
            group(0, 0, 0, True)
            group(1, 0, 1, True)
            with sp.Fori(1, n_grp // 2) as it:
                for par in range(2):
                    group(2 * it + par, it, par, False)

        @block.gpsimd
        def _(pool):
            for g in range(n_grp):
                par, it = g % 2, g // 2
                reached(pool, group_done[par], it)
                for n in range(GRP):
                    pool.wait_ge(vhi_ready[n], g + 1)
                    pool.tensor_tensor(v_lo[:, par, n, :], v_raw[:, n, :], v_hi[:, par, n, :].bitcast(F32), ALU.subtract)\
                        .then_inc(vlo_ready[n], 1)
                for k in range(V_RING):
                    reached(pool, row_added[k], g)
                    pool.indirect_dma_start(rows[:, k, :], None, v_rows, bass.IndirectOffsetOnAxis(ap=v_row[:, g * V_RING + k:g * V_RING + k + 1], axis=0),
                                            bounds_check=NK * NK - 1).then_inc(row_loaded[k], 16)

        @block.scalar
        def _(act):
            def high_parts(it):
                for par in range(2):
                    reached(act, group_done[par], it)
                    reached(act, wlo_ready[par], it)
                    act.wait_ge(wg_ready[par], it + 1)
                    act.copy(w_hi[:, par, :, :], a_in[:, par, :, :]).then_inc(whi_ready[par], 1)
                    for n in range(GRP):
                        act.wait_ge(v_loaded[n], 32 * it + 16 * par + 16)
                        act.copy(v_hi[:, par, n, :], v_raw[:, n, :]).then_inc(vhi_ready[n], 1)

            high_parts(0)
            with act.Fori(1, n_grp // 2) as it:
                high_parts(it)

        @block.tensor
        def _(pe):
            def products(it):
                for par in range(2):
                    pe.wait_ge(wlo_ready[par], it + 1)
                    for n in range(GRP):
                        pe.wait_ge(vlo_ready[n], 2 * it + par + 1)
                    for o in range(OUTS):
                        t, half = o // 2, o % 2
                        reached(pe, out_added[o], 2 * it + par)
                        for n in range(GRP):
                            for m, (ww, vv) in enumerate(((w_hi, v_hi), (w_hi, v_lo), (w_lo, v_hi))):
                                last = pe.matmul(ps[:, o, :], ww[:, par, n, t * P:(t + 1) * P], vv[:, par, n, half * 512:(half + 1) * 512],
                                                 start=(n == 0 and m == 0), stop=(n == GRP - 1 and m == 2))
                        last.then_inc(out_ready[par][o], 1)

            products(0)
            with pe.Fori(1, n_grp // 2) as it:
                products(it)

        @block.vector
        def _(dve):
            def weights(it, par):
                dve.wait_ge(in_loaded[par], 32 * it + 32)
                a4 = a_in[:, par, :, :].rearrange("p i (g t) -> p i g t", t=GT)
                g4 = g_in[:, par, :, :, :].rearrange("p g i t -> p i g t")
                dve.tensor_tensor(a4, a4, g4, ALU.mult).then_inc(wg_ready[par], 1)

            def low(it, par):
                dve.wait_ge(whi_ready[par], it + 1)
                dve.tensor_tensor(w_lo[:, par, :, :], a_in[:, par, :, :], w_hi[:, par, :, :].bitcast(F32), ALU.subtract).then_inc(wlo_ready[par], 1)

            def add(it, par, o):
                hv = h[:, 1 + o // 2, (o % 2) * 512:(o % 2) * 512 + 512]
                dve.wait_ge(out_ready[par][o], it + 1)
                reached(dve, out_added[o], 2 * it + par)
                dve.tensor_tensor(hv, hv, ps[:, o, :], ALU.add).then_inc(out_added[o], 1)

            def row(it, par, k):
                dve.wait_ge(row_loaded[k], 32 * it + 16 * par + 16)
                if k:
                    dve.wait_ge(row_added[k - 1], 2 * it + par + 1)
                else:
                    reached(dve, row_added[V_RING - 1], 2 * it + par)
                c = (2 * it + par) * V_RING + k
                w = w0[:, c:c + 1] if isinstance(it, int) else w0[:, bass.ds(it * (2 * V_RING) + (par * V_RING + k), 1)]
                dve.scalar_tensor_tensor(h[:, 0, :], rows[:, k, :], w, h[:, 0, :], ALU.mult, ALU.add).then_inc(row_added[k], 1)

            def groups(it, final):
                for par in range(2):
                    if not (final and par == 1):
                        weights(it + par, 1 - par)
                        low(it + par, 1 - par)
                    for o in range(OUTS):
                        add(it, par, o)
                        if o < V_RING:
                            row(it, par, o)

            weights(0, 0)
            low(0, 0)
            dve.wait_ge(h_loaded, 16 * TB)
            groups(0, False)
            with dve.Fori(1, n_grp // 2 - 1) as it:
                groups(it, False)
            groups(n_grp // 2 - 1, True)
    new_sem.free()


def embedding(nc, shared, io, out):
    h, con, cols = (shared[k] for k in ("h", "con", "cols"))
    PC = PLE // P
    new_sem = Semaphores(nc)
    with ExitStack() as ctx:
        sb = lambda n, s, d=F32: ctx.enter_context(nc.sbuf_tensor(n, s, d))
        names = ["p_loaded", "g_loaded", "pT_ready", "e_ready", "e_scaled", "sumsq_ready", "ms_ready", "root_ready", "xn_ready",
                 "turned_ready", "nT_ready", "gate_ready", "added", "stored", "pe_tile", "act_line", "dve_line", "wp_loaded"]
        sem = {n: new_sem("e_" + n) for n in names}
        psum = ctx.enter_context(nc.psum_tensor("e_psum", [P, 8, 512], F32))
        tiles = [(("pT", c), "pT_ready", c + 1) for c in range(PC)]
        tiles += [(("e", i), "e_ready", 2 * i + 2) for i in range(2 * TB)]
        tiles += [(("nT", c), "turned_ready", c + 1) for c in range(DC)]
        tiles += [(("g", i), "gate_ready", i + 1) for i in range(4 * TB)]
        bank = Banks(psum, tiles, sem, sem["pe_tile"])
        weights = Weights(sb, new_sem, "e", 4)
        wp = sb("e_wp", [P, PC, D])
        pin = sb("e_p", [P, TB, PLE])
        pT = sb("e_pT", [P, PC, T])
        e = sb("e_e", [P, TB, D])
        xn = sb("e_xn", [P, TB, D])
        turned = sb("e_turned", [P, 2, T])
        nT_hi = sb("e_nT_hi", [P, DC, T], F32R)
        nT_lo = sb("e_nT_lo", [P, DC, T], F32R)
        nT = (nT_hi, nT_lo)
        gain = sb("e_gain", [P, D])
        gate = sb("e_gate", [P, 4 * TB, 256])
        junk = sb("e_junk", [P, 512])
        st = sb("e_st", [P, 8, 8])
        ident = con[:, K_ID:K_ID + P]
        block = ctx.enter_context(nc.Block())

        @block.sync
        def _(sp):
            sp.dma_start(pin[:, :, :], io["p"].rearrange("(t p) d -> p t d", p=P)).then_inc(sem["p_loaded"], 16)
            sp.dma_start(wp[:, :, :], io["w_ple"].rearrange("p (c n) -> p c n", c=PC)).then_inc(sem["wp_loaded"], 16)
            sp.dma_start(gain[:, :], io["ple_gain"]).then_inc(sem["g_loaded"], 16)
            for n in range(4):
                weights.load(sp, n, io["w_gate"][n])
            for half in range(2):
                for t in range(TB):
                    sp.wait_ge(sem["added"], (2 * half + 1) * TB + t + 1)
                    sp.dma_start(out[t * P:(t + 1) * P, half * 512:(half + 1) * 512], h[:, t, half * 512:(half + 1) * 512])\
                        .then_inc(sem["stored"], 16)
            sp.wait_ge(sem["stored"], 16 * 2 * TB)

        @block.gpsimd
        def _(pool):
            weights.cut(pool)

        @block.tensor
        def _(pe):
            pe.wait_ge(sem["p_loaded"], 16)
            for c in range(PC):
                out_ = bank.take(pe, "pT", c)
                for t in range(TB):
                    last = pe.transpose(out_[:, t * P:(t + 1) * P], pin[:, t, c * P:(c + 1) * P], ident)
                last.then_inc(sem["pe_tile"], 1)
            pe.wait_ge(sem["pT_ready"], PC)
            pe.wait_ge(sem["wp_loaded"], 16)
            for i in range(2 * TB):
                t, half = i // 2, i % 2
                out_ = bank.take(pe, "e", i)
                for c in range(PC):
                    last = pe.matmul(out_, pT[:, c, t * P:(t + 1) * P], wp[:, c, half * 512:(half + 1) * 512], start=(c == 0), stop=(c == PC - 1))
                last.then_inc(sem["pe_tile"], 1)
            pe.wait_ge(sem["xn_ready"], TB)
            for c in range(DC):
                out_ = bank.take(pe, "nT", c)
                for t in range(TB):
                    last = pe.transpose(out_[:, t * P:(t + 1) * P], xn[:, t, c * P:(c + 1) * P], ident)
                last.then_inc(sem["pe_tile"], 1)
            pe.wait_ge(sem["nT_ready"], DC)
            for n in range(4):
                w = weights.ready(pe, n)
                for t in range(TB):
                    out_ = bank.take(pe, "g", n * TB + t)[:, 0:256]
                    last = product(pe, out_, lambda part, d: nT[part][:, d, t * P:(t + 1) * P], lambda part, d: w[part][:, d, :])
                    last.then_inc(sem["pe_tile"], 1)
                pe.drain().then_inc(weights.used[n % 2], 1)

        @block.scalar
        def _(act):
            me = Line(act, sem["act_line"])
            for t in range(TB):
                me.did(act.activation(xn[:, t, :], h[:, t, :], ACT.Square, accum_out=st[:, 0, t:t + 1]), sem["sumsq_ready"])
            act.wait_ge(sem["ms_ready"], 1)
            me.did(act.activation(st[:, 2, 0:TB], st[:, 1, 0:TB], ACT.Sqrt), sem["root_ready"])
            for c in range(PC):
                src = bank.filled(act, "pT", c)
                me.did(act.copy(pT[:, c, :], src), sem["pT_ready"])
            for i in range(2 * TB):
                t, half = i // 2, i % 2
                src = bank.filled(act, "e", i)
                me.did(act.copy(e[:, t, half * 512:(half + 1) * 512], src), sem["e_ready"])
                me.settle()
                me.did(act.activation(junk[:, :], src, ACT.Square, accum_out=st[:, 4, i:i + 1]), sem["e_ready"])
            act.wait_ge(sem["ms_ready"], 2)
            me.did(act.activation(st[:, 6, 0:TB], st[:, 5, 0:TB], ACT.Sqrt), sem["root_ready"])
            for c in range(DC):
                src = bank.filled(act, "nT", c)
                if c >= 2:
                    act.wait_ge(sem["nT_ready"], c - 1)
                me.did(act.activation(turned[:, c % 2, :], src, ACT.Copy, scale=col(cols, C_GATE + c)), sem["turned_ready"])
            for i in range(4 * TB):
                src = bank.filled(act, "g", i)[:, 0:256]
                me.did(act.activation(gate[:, i, :], src, ACT.Sigmoid), sem["gate_ready"])

        @block.vector
        def _(dve):
            me = Line(dve, sem["dve_line"])

            def step(ins, s=None):
                me.did(ins, s)
                me.settle()

            dve.wait_ge(sem["sumsq_ready"], TB)
            step(dve.tensor_scalar(st[:, 1, 0:TB], st[:, 0, 0:TB], 1.0 / D, EPS, ALU.mult, ALU.add), sem["ms_ready"])
            dve.wait_ge(sem["root_ready"], 1)
            step(dve.reciprocal(st[:, 3, 0:TB], st[:, 2, 0:TB]))
            for t in range(TB):
                me.did(dve.tensor_scalar(xn[:, t, :], h[:, t, :], st[:, 3, t:t + 1], None, ALU.mult), sem["xn_ready"])
            dve.wait_ge(sem["e_ready"], 4 * TB)
            step(dve.tensor_reduce(st[:, 7, 0:TB], st[:, 4, :].rearrange("p (t a) -> p t a", a=2), AX.X, ALU.add))
            step(dve.tensor_scalar(st[:, 5, 0:TB], st[:, 7, 0:TB], 1.0 / D, EPS, ALU.mult, ALU.add), sem["ms_ready"])
            for c in range(DC):
                dve.wait_ge(sem["turned_ready"], c + 1)
                step(dve.tensor_copy(nT_hi[:, c, :], turned[:, c % 2, :]))
                me.did(dve.tensor_tensor(nT_lo[:, c, :], turned[:, c % 2, :], nT_hi[:, c, :].bitcast(F32), ALU.subtract), sem["nT_ready"])
            dve.wait_ge(sem["root_ready"], 2)
            step(dve.reciprocal(st[:, 7, 4:8], st[:, 6, 0:TB]))
            dve.wait_ge(sem["g_loaded"], 16)
            for t in range(TB):
                me.did(dve.scalar_tensor_tensor(e[:, t, :], e[:, t, :], st[:, 7, 4 + t:5 + t], gain[:, :], ALU.mult, ALU.mult))
            me.settle()
            for i in range(4 * TB):
                n, t = i // TB, i % TB
                dve.wait_ge(sem["gate_ready"], i + 1)
                step(dve.tensor_tensor(gate[:, i, :], gate[:, i, :], e[:, t, n * 256:(n + 1) * 256], ALU.mult))
                hv = h[:, t, n * 256:(n + 1) * 256]
                me.did(dve.tensor_tensor(hv, hv, gate[:, i, :], ALU.add), sem["added"])
    new_sem.free()


def block_kernel(nc, io, out):
    act_dram = nc.dram_tensor("act_scratch", [NK, P, DT], F32, kind="Internal").ap()
    gate_dram = nc.dram_tensor("gate_scratch", [DT // GT, P, NK, GT], F32, kind="Internal").ap()
    h_dram = nc.dram_tensor("h_scratch", [TB, P, D], F32, kind="Internal").ap()
    with ExitStack() as ctx:
        sb = lambda c, n, s, d=F32: c.enter_context(nc.sbuf_tensor(n, s, d))
        shared = {"h": sb(ctx, "h", [P, TB, D]), "con": sb(ctx, "con", [P, K_END]), "cols": sb(ctx, "cols", [P, C_END])}
        mixer(nc, shared, io)
        shared["w0"], shared["v_row"] = sb(ctx, "w0", [P, PAIRS]), sb(ctx, "v_row", [P, PAIRS], U32)
        with ExitStack() as mid:
            shared["hn_hi"] = sb(mid, "hn_hi", [P, DC, T], F32R)
            shared["hn_lo"] = sb(mid, "hn_lo", [P, DC, T], F32R)
            shared["scores"] = sb(mid, "scores", [P, TB, LISTS, NK])
            retrieval(nc, shared, io, h_dram)
            scoring(nc, shared, io, act_dram, gate_dram)
        values(nc, shared, io, act_dram, gate_dram, h_dram)
        embedding(nc, shared, io, out)


def constants():
    con = np.zeros((P, K_END), np.float32)
    i = np.arange(P)
    con[:, K_ID:K_ID + P] = i[:, None] == i[None, :]
    con[:, K_TRI:K_TRI + P] = i[:, None] <= i[None, :]
    con[:, K_NEG:K_NEG + P] = np.where(i[:, None] > i[None, :], NEG, 0.0)
    con[:, K_IOTA:K_IOTA + P] = i[None, :]
    con[:, K_URO:K_URO + P] = i[None, :] < CHUNK
    con[:, K_NRO:K_NRO + CHUNK] = NEG
    con[:, K_INV:K_INV + HD // 2] = 1.0 / (10000.0 ** (np.arange(0, HD, 2) / HD)).astype(np.float32)
    return con


def by_feature(g):
    g = np.asarray(g)
    n = g.shape[0] // P
    return np.ascontiguousarray(g.reshape(n, P, -1).transpose(1, 0, 2).reshape(P, -1))


def weight_tiles(w, width=Weights.WIDTH):
    return np.ascontiguousarray(np.stack([by_feature(w[:, a:a + width]) for a in range(0, w.shape[1], width)]))


def kernel(**inputs):
    from concourse import bacc
    from concourse.bass_utils import run_bass_kernel_spmd

    a = {k: np.asarray(v) for k, v in inputs.items()}
    one = {k: v[0] for k, v in a.items() if k not in ("x", "positions")}
    w_in = one["w_in"]
    z0, x0, t0, q0 = 0, SSD_W, SSD_W + 1024, SSD_W + 1024 + SSD_H
    cut = [w_in[:, x0:x0 + 1024], w_in[:, q0:q0 + 1536], w_in[:, z0:z0 + 512]]
    line = np.concatenate([one["dt_bias"], one["a_log"], one["d_skip"], one["q_norm_g"], one["k_norm_g"], one["lam_vecs"].reshape(-1),
                           one["diff_norm_g"], one["ssd_norm_g"]])
    arrays = {
        "x": a["x"][0], "positions": a["positions"].reshape(TB, P).T, "p": one["p"][0],
        "consts": constants(),
        "rows": np.ascontiguousarray(np.broadcast_to(line, (P, R_END))),
        "cols": np.concatenate([by_feature(one["norm_mix_g"][:, None]), by_feature(one["norm_ffn_g"][:, None]),
                                by_feature(one["ple_gate_norm_g"][:, None]), by_feature(one["conv_w"].T),
                                by_feature(one["conv_b"][:, None])], axis=1),
        "w_in": weight_tiles(np.concatenate(cut, axis=1)),
        "w_dt": by_feature(w_in[:, t0:q0]),
        "w_out": weight_tiles(one["w_out"]),
        "w_q": weight_tiles(one["peer_wq"]),
        "keys": np.concatenate([one["peer_k1"].T, one["peer_k2"].T], axis=1),
        "u_t": one["peer_u"].reshape(NK, NK, DC, P).transpose(1, 3, 2, 0).reshape(NK, P, DC * P),
        "v_t": one["peer_v"].reshape(NK, NK, D).transpose(1, 0, 2),
        "u_rows": one["peer_u"],
        "ffn_gain": np.broadcast_to(one["norm_ffn_g"], (P, D)),
        "w_ple": by_feature(one["ple_proj"]),
        "ple_gain": np.broadcast_to(one["ple_norm_g"], (P, D)),
        "w_gate": weight_tiles(one["ple_gate_w"]),
    }
    arrays = {f"in_{k}": np.ascontiguousarray(v) for k, v in arrays.items()}
    nc = bacc.Bacc("TRN2", target_bir_lowering=False, num_devices=1)
    io = {k[3:]: nc.dram_tensor(k, v.shape, mybir.dt.from_np(v.dtype), kind="ExternalInput").ap() for k, v in arrays.items()}
    out = nc.dram_tensor("out_h", (T, D), F32, kind="ExternalOutput").ap()
    block_kernel(nc, io, out)
    r = run_bass_kernel_spmd(nc, [arrays], core_ids=[0])
    return r.results[0]["out_h"].reshape(1, T, D)
```

```python
import math
from contextlib import ExitStack

import numpy as np

import concourse.bass as bass
from concourse import mybir

F32 = mybir.dt.float32
F32R = mybir.dt.float32r
I32 = mybir.dt.int32
U32 = mybir.dt.uint32
ALU = mybir.AluOpType
ACT = mybir.ActivationFunctionType
AX = mybir.AxisListType

P = 128
T = 512
D = 1024
TB = T // P
DC = D // P
HD = 64
SSD_H, SSD_G, SSD_N, SSD_W = 8, 2, 128, 512
HPG = SSD_H // SSD_G
TAPS = 4
DIFF_H = 4
CHUNK = 64
XBC_C = 1024 // P
PH, NK, TOPK = 8, 128, 16
LISTS = 2 * PH
PAIRS = PH * TOPK
ROW_LEN = [TOPK // (i + 1) for i in range(TOPK)]
CAND = sum(ROW_LEN)
LONG_ROWS = sum(n > 1 for n in ROW_LEN)
PLE = 256
EPS = 1e-6
LAM_INIT = 0.2
NEG = -1e30
LOWEST = -3.0e38
MAGIC = 12582912.0

PI2_A = 6.28125
PI2_B = 2029.0 / 2**20
PI2_C = 2 * math.pi - PI2_A - PI2_B
INV_2PI = 1.0 / (2 * math.pi)

K_ID, K_TRI, K_NEG, K_IOTA, K_URO, K_NRO, K_INV = 0, 128, 256, 384, 512, 640, 704
K_END = 736
R_DTB, R_ALOG, R_DSK, R_QG, R_KG, R_LAM, R_DG, R_SG = 0, 8, 16, 24, 88, 152, 408, 536
R_END = 1048
C_MIX, C_FFN, C_GATE, C_CW, C_CB = 0, 8, 16, 24, 56
C_END = 64

UR = 4
GT = 32
STEP_TOK = 8
LOOP_A = 72
EXP_AT, TURN_AT = 64, 68
FIRST_GATHER = 12
DT = T - P
U_RING = 4
DOTS_1, DOTS_T, DOTS_J = 3, 16, 12
DOT_AT = (1, 2, 3, 4, 5, 6, 8, 9, 11, 12, 14, 16, 17, 19, 20, 22)


def reached(eng, sem, value):
    if not (isinstance(value, int) and value <= 0):
        eng.wait_ge(sem, value)


class Line:

    def __init__(self, eng, sem):
        self.eng, self.sem, self.count, self.last = eng, sem, {}, None

    def did(self, ins, sem=None):
        sem = sem or self.sem
        n = self.count[id(sem)] = self.count.get(id(sem), 0) + 1
        ins.then_inc(sem, 1)
        self.last = (sem, n)

    def settle(self):
        self.eng.wait_ge(*self.last)


def col(ap, i):
    return ap[:, i:i + 1]


def spread_last(ap, n):
    return ap.unsqueeze(len(ap.shape)).to_broadcast([*ap.shape, n])


class Semaphores:

    def __init__(self, nc):
        self.nc, self.all = nc, []

    def __call__(self, name):
        self.all.append(self.nc.alloc_semaphore(name))
        return self.all[-1]

    def free(self):
        self.nc.clear_and_free_semaphores(self.all)
        self.nc.all_engine_barrier()


class Weights:

    WIDTH = 256

    def __init__(self, sb, new_sem, tag, count):
        self.count = count
        self.raw = sb(f"{tag}_w_raw", [P, 2, DC, self.WIDTH])
        self.hi = sb(f"{tag}_w_hi", [P, 2, DC, self.WIDTH], F32R)
        self.lo = sb(f"{tag}_w_lo", [P, 2, DC, self.WIDTH], F32R)
        self.loaded, self.hi_ready, self.lo_ready, self.used = (
            [new_sem(f"{tag}_w_{n}{i}") for i in range(2)] for n in ("loaded", "hi_ready", "lo_ready", "used"))

    def load(self, sp, n, src):
        if n >= 2:
            sp.wait_ge(self.lo_ready[n % 2], n // 2)
        sp.dma_start(self.raw[:, n % 2, :, :], src.rearrange("p (c n) -> p c n", c=DC)).then_inc(self.loaded[n % 2], 16)

    def cut(self, pool):
        for n in range(self.count):
            s = n % 2
            pool.wait_ge(self.loaded[s], 16 * (n // 2 + 1))
            if n >= 2:
                pool.wait_ge(self.used[s], n // 2)
            pool.tensor_scalar(self.hi[:, s, :, :], self.raw[:, s, :, :], 1.0, 1.0, ALU.mult, ALU.mult).then_inc(self.hi_ready[s], 1)
            pool.wait_ge(self.hi_ready[s], n // 2 + 1)
            pool.tensor_tensor(self.lo[:, s, :, :], self.raw[:, s, :, :], self.hi[:, s, :, :].bitcast(F32), ALU.subtract)\
                .then_inc(self.lo_ready[s], 1)

    def ready(self, pe, n):
        pe.wait_ge(self.lo_ready[n % 2], n // 2 + 1)
        return self.hi[:, n % 2, :, :], self.lo[:, n % 2, :, :]


def product(pe, out, left, right, made=None):
    n_blocks = DC
    for d in range(n_blocks):
        if made:
            pe.wait_ge(made[0], made[1] + d + 1)
        pe.matmul(out, left(0, d), right(0, d), start=(d == 0), stop=False)
        pe.matmul(out, left(0, d), right(1, d), start=False, stop=False)
        last = pe.matmul(out, left(1, d), right(0, d), start=False, stop=(d == n_blocks - 1))
    return last


def turn_blocks(pe, bank, name, made, per_block, src, ident):
    outs = [bank.take(pe, name, c) for c in range(DC)]
    for t in range(TB):
        pe.wait_ge(made, per_block * (t + 1))
        for c in range(DC):
            last = pe.transpose(outs[c][:, t * P:(t + 1) * P], src(t, c), ident)
            if t == TB - 1:
                last.then_inc(bank.done, 1)


def mixer_tiles():
    out = []
    out += [(("xT", c), "nT_ready", c + 1) for c in range(DC)]
    out += [(("xbc", c), "conv_done", c + 1) for c in range(XBC_C)]
    out += [(("dtT", 0), "dtT_ready", 1)]
    for name, ready in (("q", "qk_roped"), ("v", "v_ready"), ("k", "qk_roped")):
        base = 2 * TB if name == "k" else 0
        out += [((name, i), ready, base + i + 1) for i in range(2 * TB)]
        if name == "q":
            out.insert(-2 * TB + 1, (("dt", 0), "dtraw_done", 1))
    for t in range(TB):
        out += [(("xsT", t), "xs_ready", t + 1), (("bT", t), "btok_ready", t + 1)]
    for t in range(TB):
        out += [(("cs", t), "ncs_ready", t + 1)]
        out += [(("csb", t, g), "decay_ready", 2 * t + g + 1) for g in range(SSD_G)]
        out += [(("cb", t), "m_ready", 2 * t + 2)]
        out += [(("z", half * TB + t), "z_copied", 2 * t + half + 1) for half in range(2)]
        out += [(("y", t), "y_ready", t + 1)]
        if t:
            out += [(("yo", t), "y_ready", t + 1)]
        if t < TB - 1:
            out += [(("st", t), "state_ready", t + 1)]
        if t == 1:
            out += [(("qkT", i), "qkT_ready", i + 1) for i in range(2 * DIFF_H)]
    units = TB * DIFF_H
    for i in range(units + 2):
        if i < units:
            out += [(("s", i, c), "probs_ready", 2 * i + c + 1) for c in range(2)]
        if 0 <= i - 1 < units:
            out += [(("aT", i - 1), "attnT_ready", i)]
        if 0 <= i - 2:
            out += [(("o", i - 2), "o_ready", i - 1)]
    out += [(("yT", c), "nT_ready", DC + c + 1) for c in range(DC)]
    out += [(("h", i), "h_ready", i + 1) for i in range(4 * TB)]
    return out


class Banks:

    def __init__(self, psum, tiles, sems, done):
        self.psum, self.sems, self.done = psum, sems, done
        self.index = {name: n for n, (name, _, _) in enumerate(tiles)}
        self.frees = [(s, v) for _, s, v in tiles]
        self.n = psum.shape[1]

    def at(self, *name):
        return self.psum[:, self.index[name] % self.n, :]

    def take(self, pe, *name):
        i = self.index[name] - self.n
        if i >= 0:
            s, v = self.frees[i]
            pe.wait_ge(self.sems[s], v)
        return self.at(*name)

    def filled(self, eng, *name):
        eng.wait_ge(self.done, self.index[name] + 1)
        return self.at(*name)


def mixer(nc, shared, io):
    h = shared["h"]
    con, cols = shared["con"], shared["cols"]
    N_IN = 12
    new_sem = Semaphores(nc)
    with ExitStack() as ctx:
        sb = lambda n, s, d=F32: ctx.enter_context(nc.sbuf_tensor(n, s, d))
        names = ["high_ready", "nT_ready", "x_again", "wdt_hi_ready", "wdt_lo_ready", "conv_done", "dtT_ready", "dtraw_done", "qk_roped", "v_ready", "z_copied", "z_ready", "qkT_ready", "xs_ready",
                 "btok_ready", "ncs_ready", "decay_ready", "m_ready", "y_ready", "state_ready", "probs_ready",
                 "attnT_ready", "o_ready", "h_ready", "const_loaded", "dtw_loaded", "pe_tile", "act_line",
                 "dve_line", "sumsq_ready", "ms_ready", "root_ready", "xn_ready", "sine_asked", "sine_ready",
                 "qksq_ready", "qkms_ready", "qkroot_ready", "qk_ready", "xbc_ready", "abs_ready", "edt_ready",
                 "dt_asked", "lam_asked", "lam_exp", "xdt_ready", "ecs_ready", "attn_ready", "bias_ready",
                 "fin_sq", "fin_ms", "fin_root", "mix_ready", "aexp_ready", "alog_go"]
        sem = {n: new_sem("m_" + n) for n in names}
        x_loaded = [new_sem(f"m_x_loaded{t}") for t in range(TB)]
        psum = ctx.enter_context(nc.psum_tensor("m_psum", [P, 8, 512], F32))
        bank = Banks(psum, mixer_tiles(), sem, sem["pe_tile"])

        weights = Weights(sb, new_sem, "m", N_IN + 4)
        wdt = sb("m_wdt", [P, DC, SSD_H])
        wdt_hi = sb("m_wdt_hi", [P, DC, SSD_H], F32R)
        wdt_lo = sb("m_wdt_lo", [P, DC, SSD_H], F32R)
        rows = sb("m_rows", [P, R_END])
        nT_hi = sb("m_nT_hi", [P, DC, T], F32R)
        nT_lo = sb("m_nT_lo", [P, DC, T], F32R)
        nT = (nT_hi, nT_lo)
        mix = h
        xbcT = sb("m_xbcT", [P, XBC_C, T])
        zs = sb("m_zs", [P, TB, SSD_W])
        v = sb("m_v", [P, TB, 512])
        qkT = sb("m_qkT", [P, 2 * DIFF_H, T])
        xs = sb("m_xs", [P, TB, SSD_W])
        btok = sb("m_btok", [P, TB, SSD_G * SSD_N])
        tab = sb("m_tab", [P, 4, TB, 2, HD // 2])
        ang = sb("m_ang", [P, 5, TB, HD // 2])
        x_in = xbcT[:, :, :].rearrange("p c t -> p (c t)").rearrange("p (t d) -> p t d", t=TB)
        posf = sb("m_posf", [P, TB])
        posi = sb("m_posi", [P, TB], I32)
        small = sb("m_small", [P, 64])
        ropeA = sb("m_ropeA", [P, 2, 512])
        ropeB = sb("m_ropeB", [P, 2, 512])
        dtT = ropeB[0:SSD_H, 0, :]
        qn = sb("m_qn", [P, TB, 2, 512])
        dts = sb("m_dts", [P, 8, TB, SSD_H])
        state = sb("m_state", [P, SSD_W])
        dec = sb("m_dec", [P, 2, HPG, P])
        ecl = sb("m_ecl", [P, SSD_H])
        Mt = tab[:, :, :, :, :].rearrange("p a t b c -> p (a t b c)").rearrange("p (h l) -> p h l", l=P)
        xdt = sb("m_xdt", [P, SSD_W])
        xdtd = sb("m_xdtd", [P, SSD_W])
        st8 = sb("m_st8", [P, 64])
        prob = qn[:, :, 1, :].rearrange("p (u c) n -> p u c n", u=2)
        attn = xbcT[:, 0:2, :]
        attnT = xbcT[:, 2:4, :].rearrange("p u (k q) -> p u k q", q=P)
        red = sb("m_red", [P, 8, 8])
        fin = sb("m_fin", [P, 4, 32])
        sqj = dec[:, 0, :, :].rearrange("p a b -> p (a b)")

        ident = con[:, K_ID:K_ID + P]
        ss, ms, root, rstd = (small[:, 4 * i:4 * i + 4] for i in range(4))
        ssq, msq, rootq, rstdq = (fin[:, i, :] for i in range(4))
        qks = sb("m_qks", [P, 4, 4 * TB, 4])
        X_DT, X_NA, X_DA, X_NCS, X_ECS, X_A, X_B, X_C = range(8)
        a_rate = small[:, 16:24]
        lam = small[:, 24:30]
        qT = lambda hh: qkT[:, hh, :]
        kT = lambda hh: qkT[:, DIFF_H + hh, :]
        units = [(b, hh) for b in range(TB) for hh in range(DIFF_H)]

        block = ctx.enter_context(nc.Block())

        @block.sync
        def _(sp):
            for t in (0, 2, 1, 3):
                sp.dma_start(x_in[:, t, :], io["x"][t * P:(t + 1) * P, :]).then_inc(x_loaded[t], 16)
            sp.dma_start(con[:, :], io["consts"]).then_inc(sem["const_loaded"], 16)
            sp.dma_start(cols[:, :], io["cols"]).then_inc(sem["const_loaded"], 16)
            sp.dma_start(rows[:, :], io["rows"]).then_inc(sem["const_loaded"], 16)
            sp.dma_start(posi[:, :], io["positions"]).then_inc(sem["const_loaded"], 16)
            sp.dma_start(wdt[:, :, :], io["w_dt"].rearrange("p (c n) -> p c n", c=DC)).then_inc(sem["dtw_loaded"], 16)
            for n in range(N_IN):
                weights.load(sp, n, io["w_in"][n])
            for n in range(4):
                weights.load(sp, N_IN + n, io["w_out"][n])
            sp.wait_ge(sem["pe_tile"], bank.index[("yT", DC - 1)] + 1)
            for t in range(TB):
                sp.dma_start(h[:, t, :], io["x"][t * P:(t + 1) * P, :]).then_inc(sem["x_again"], 16)

        @block.gpsimd
        def _(pool):
            pool.wait_ge(sem["dtw_loaded"], 16)
            pool.tensor_copy(wdt_hi[:, :, :], wdt[:, :, :]).then_inc(sem["wdt_hi_ready"], 1)
            pool.wait_ge(sem["wdt_hi_ready"], 1)
            pool.tensor_tensor(wdt_lo[:, :, :], wdt[:, :, :], wdt_hi[:, :, :].bitcast(F32), ALU.subtract).then_inc(sem["wdt_lo_ready"], 1)
            weights.cut(pool)

        @block.tensor
        def _(pe):
            def tile_done(ins):
                ins.then_inc(sem["pe_tile"], 1)

            pe.wait_ge(sem["const_loaded"], 64)
            turn_blocks(pe, bank, "xT", sem["xn_ready"], 1, lambda t, c: mix[:, t, c * P:(c + 1) * P], ident)
            for c in range(XBC_C):
                w = weights.ready(pe, c // 2)
                out = bank.take(pe, "xbc", c)
                tile_done(product(pe, out, lambda part, d: w[part][:, d, (c % 2) * P:(c % 2 + 1) * P], lambda part, d: nT[part][:, d, :],
                                  made=(sem["nT_ready"], 0) if c == 0 else None))
                if c % 2:
                    pe.drain().then_inc(weights.used[c // 2 % 2], 1)
            pe.wait_ge(sem["wdt_lo_ready"], 1)
            out = bank.take(pe, "dtT", 0)
            wd = (wdt_hi, wdt_lo)
            tile_done(product(pe, out[0:SSD_H, :], lambda part, d: wd[part][:, d, :], lambda part, d: nT[part][:, d, :]))

            def project(n, name, half, t):
                w = weights.ready(pe, n)
                out = bank.take(pe, name, half * TB + t)[:, 0:256]
                tile_done(product(pe, out, lambda part, d: nT[part][:, d, t * P:(t + 1) * P], lambda part, d: w[part][:, d, :]))

            for n in range(XBC_C // 2, N_IN - 2):
                for t in range(TB):
                    project(n, "qvk"[(n - 4) // 2], n % 2, t)
                    if n == XBC_C // 2 and t == 0:
                        pe.wait_ge(sem["dtT_ready"], 1)
                        out = bank.take(pe, "dt", 0)
                        for b in range(TB):
                            last = pe.transpose(out[:, b * 8:b * 8 + 8], dtT[:, b * P:(b + 1) * P], ident[0:SSD_H, 0:SSD_H])
                        tile_done(last)
                pe.drain().then_inc(weights.used[n % 2], 1)
            pe.wait_ge(sem["xbc_ready"], XBC_C)
            for t in range(TB):
                out = bank.take(pe, "xsT", t)
                for c in range(4):
                    last = pe.transpose(out[:, c * P:(c + 1) * P], xbcT[:, c, t * P:(t + 1) * P], ident)
                tile_done(last)
                out = bank.take(pe, "bT", t)
                for c in range(SSD_G):
                    last = pe.transpose(out[:, c * P:(c + 1) * P], xbcT[:, 4 + c, t * P:(t + 1) * P], ident)
                tile_done(last)
            pe.wait_ge(sem["dt_asked"], 1)
            tri, neg = con[:, K_TRI:K_TRI + P], con[:, K_NEG:K_NEG + P]
            for t in range(TB):
                tok = slice(t * P, (t + 1) * P)
                out = bank.take(pe, "cs", t)
                tile_done(pe.matmul(out[:, 0:SSD_H], tri, dts[:, X_DA, t, :], start=True, stop=True))
                for g in range(SSD_G):
                    out = bank.take(pe, "csb", t, g)
                    for r in range(HPG):
                        da = dts[:, X_DA, t, g * HPG + r:g * HPG + r + 1]
                        pe.matmul(out[:, r * P:(r + 1) * P], da.to_broadcast([P, P]), tri, start=True, stop=False)
                        last = pe.matmul(out[:, r * P:(r + 1) * P], ident, neg, start=False, stop=True)
                    tile_done(last)
                out = bank.take(pe, "cb", t)
                for g in range(SSD_G):
                    last = pe.matmul(out[:, g * P:(g + 1) * P], xbcT[:, 4 + g, tok], xbcT[:, 6 + g, tok], start=True, stop=True)
                tile_done(last)
                for half in range(2):
                    project(N_IN - 2 + half, "z", half, t)
                    if t == TB - 1:
                        pe.drain().then_inc(weights.used[half], 1)
                pe.wait_ge(sem["xdt_ready"], 2 * t + 1)
                pe.wait_ge(sem["m_ready"], 2 * t + 2)
                out = bank.take(pe, "y", t)
                for hh in range(SSD_H):
                    last = pe.matmul(out[:, hh * HD:(hh + 1) * HD], Mt[:, hh, :], xdt[:, hh * HD:(hh + 1) * HD], start=True, stop=True)
                tile_done(last)
                if t:
                    pe.wait_ge(sem["state_ready"], t)
                    out = bank.take(pe, "yo", t)
                    for g in range(SSD_G):
                        last = pe.matmul(out[:, g * 256:(g + 1) * 256], xbcT[:, 6 + g, tok], state[:, g * 256:(g + 1) * 256], start=True, stop=True)
                    tile_done(last)
                if t < TB - 1:
                    pe.wait_ge(sem["btok_ready"], t + 1)
                    pe.wait_ge(sem["xdt_ready"], 2 * t + 2)
                    out = bank.take(pe, "st", t)
                    for g in range(SSD_G):
                        last = pe.matmul(out[:, g * 256:(g + 1) * 256], btok[:, t, g * P:(g + 1) * P], xdtd[:, g * 256:(g + 1) * 256], start=True, stop=True)
                    tile_done(last)
                if t == 1:
                    pe.wait_ge(sem["qk_ready"], 4 * TB)
                    for i in range(2 * DIFF_H):
                        out = bank.take(pe, "qkT", i)
                        which, hh = i // DIFF_H, i % DIFF_H
                        for b in range(TB):
                            last = pe.transpose(out[:, b * P:(b + 1) * P], qn[:, b, which, hh * P:(hh + 1) * P], ident)
                        tile_done(last)
            pe.wait_ge(sem["qkT_ready"], 2 * DIFF_H)
            pe.wait_ge(sem["v_ready"], 2 * TB)
            for i in range(len(units) + 2):
                if i < len(units):
                    b, hh = units[i]
                    kend = (b + 1) * P
                    for c in range(2):
                        out = bank.take(pe, "s", i, c)
                        rowsl = slice(c * HD, (c + 1) * HD)
                        pe.matmul(out[:, 0:kend], qT(hh)[rowsl, b * P:kend], kT(hh)[rowsl, 0:kend], start=True, stop=False)
                        tile_done(pe.matmul(out[:, kend - CHUNK:kend], con[0:1, K_URO:K_URO + P], con[0:1, K_NRO:K_NRO + CHUNK],
                                            start=False, stop=True))
                if 0 <= i - 1 < len(units):
                    b, hh = units[i - 1]
                    pe.wait_ge(sem["attn_ready"], i)
                    out = bank.take(pe, "aT", i - 1)
                    for kb in range(b + 1):
                        last = pe.transpose(out[:, kb * P:(kb + 1) * P], attn[:, (i - 1) % 2, kb * P:(kb + 1) * P], ident)
                    tile_done(last)
                if 0 <= i - 2:
                    b, hh = units[i - 2]
                    pe.wait_ge(sem["attnT_ready"], i - 1)
                    out = bank.take(pe, "o", i - 2)
                    for kb in range(b + 1):
                        last = pe.matmul(out[:, 0:P], attnT[:, i % 2, kb, :], v[:, kb, hh * P:(hh + 1) * P], start=(kb == 0), stop=(kb == b))
                    tile_done(last)
            turn_blocks(pe, bank, "yT", sem["mix_ready"], 2, lambda t, c: mix[:, t, c * P:(c + 1) * P], ident)
            for n in range(4):
                w = weights.ready(pe, N_IN + n)
                for t in range(TB):
                    out = bank.take(pe, "h", n * TB + t)[:, 0:256]
                    tile_done(product(pe, out, lambda part, d: nT[part][:, d, t * P:(t + 1) * P], lambda part, d: w[part][:, d, :],
                                      made=(sem["nT_ready"], DC) if n == t == 0 else None))
                pe.drain().then_inc(weights.used[n % 2], 1)

        @block.scalar
        def _(act):
            me = Line(act, sem["act_line"])
            for t in range(TB // 2):
                act.wait_ge(x_loaded[t], 16)
                me.did(act.activation(mix[:, t, :], x_in[:, t, :], ACT.Square, accum_out=col(ss, t)), sem["sumsq_ready"])
            act.wait_ge(sem["ms_ready"], 1)
            me.did(act.activation(root, ms, ACT.Sqrt), sem["root_ready"])
            act.wait_ge(sem["const_loaded"], 64)
            for c in range(DC):
                src = bank.filled(act, "xT", c)
                me.did(act.activation(nT_hi[:, c, :], src, ACT.Copy, scale=col(cols, C_MIX + c)), sem["high_ready"])
            act.wait_ge(sem["sine_asked"], 1)
            me.did(act.activation(ang[:, 3, :, :], ang[:, 0, :, :], ACT.Sin, scale=0.5), sem["sine_ready"])
            me.did(act.activation(ang[:, 4, :, :], ang[:, 0, :, :], ACT.Sin), sem["sine_ready"])
            me.did(act.copy(dtT, bank.filled(act, "dtT", 0)[0:SSD_H, :]), sem["dtT_ready"])
            act.wait_ge(sem["abs_ready"], 1)
            me.did(act.activation(dts[:, X_B, :, :], dts[:, X_A, :, :], ACT.Exp, scale=-1.0), sem["edt_ready"])
            me.did(act.activation(a_rate, rows[:, R_ALOG:R_ALOG + 8], ACT.Exp), sem["aexp_ready"])
            act.wait_ge(sem["lam_asked"], 1)
            me.did(act.activation(lam[:, 2:4], lam[:, 0:2], ACT.Exp), sem["lam_exp"])

            def square_qk(i):
                src = bank.filled(act, "qk"[i // (2 * TB)], i % (2 * TB))[:, 0:256]
                if i:
                    act.wait_ge(sem["qkms_ready"], i)
                me.did(act.activation(sqj[:, 0:256], src, ACT.Square), sem["qksq_ready"])
                act.wait_ge(sem["qkms_ready"], i + 1)
                me.did(act.activation(qks[:, 1, i, :], qks[:, 0, i, :], ACT.Sqrt), sem["qkroot_ready"])

            for i in range(2 * TB):
                square_qk(i)
            for i in range(2 * TB):
                src = bank.filled(act, "v", i)[:, 0:256]
                half, t = i // TB, i % TB
                me.did(act.copy(v[:, t, half * 256:(half + 1) * 256], src), sem["v_ready"])
            for c in range(XBC_C):
                act.wait_ge(sem["conv_done"], c + 1)
                me.did(act.activation(xbcT[:, c, :], xbcT[:, c, :], ACT.Silu), sem["xbc_ready"])
            for i in range(2 * TB, 4 * TB):
                square_qk(i)
            for t in range(TB):
                src = bank.filled(act, "xsT", t)
                me.did(act.copy(xs[:, t, :], src), sem["xs_ready"])
                src = bank.filled(act, "bT", t)
                me.did(act.copy(btok[:, t, :], src[:, 0:SSD_G * SSD_N]), sem["btok_ready"])
            for t in range(TB):
                act.wait_ge(sem["ncs_ready"], t + 1)
                me.did(act.activation(dts[:, X_ECS, t, :], dts[:, X_NCS, t, :], ACT.Exp, scale=-1.0), sem["ecs_ready"])
                for g in range(SSD_G):
                    src = bank.filled(act, "csb", t, g)
                    if t:
                        act.wait_ge(sem["m_ready"], 2 * t - 1 + g)
                        if t < TB:
                            act.wait_ge(sem["state_ready"], t)
                        act.wait_ge(sem["xdt_ready"], 2 * t)
                    for r in range(HPG):
                        hh = g * HPG + r
                        me.did(act.activation(dec[:, g, r, :], src[:, r * P:(r + 1) * P], ACT.Exp, bias=dts[:, X_NCS, t, hh:hh + 1]))
                    me.did(act.activation(ecl[:, g * HPG:(g + 1) * HPG], src.rearrange("p (r l) -> p r l", r=HPG)[:, :, P - 1], ACT.Exp),
                           sem["decay_ready"])
                for half in range(2):
                    src = bank.filled(act, "z", half * TB + t)[:, 0:256]
                    me.did(act.copy(zs[:, t, half * 256:(half + 1) * 256], src), sem["z_copied"])
                if t == 1:
                    for i in range(2 * DIFF_H):
                        src = bank.filled(act, "qkT", i)
                        me.did(act.copy(qkT[:, i, :], src), sem["qkT_ready"])
            act.wait_ge(sem["z_copied"], 2 * TB)
            for t in range(TB):
                me.did(act.activation(zs[:, t, :], zs[:, t, :], ACT.Silu), sem["z_ready"])
            for i in range(len(units) + 2):
                if i < len(units):
                    b, hh = units[i]
                    kend = (b + 1) * P
                    for c in range(2):
                        src = bank.filled(act, "s", i, c)
                        act.wait_ge(sem["bias_ready"], 2 * i + c + 1)
                        if i >= 2:
                            act.wait_ge(sem["attn_ready"], i - 1)
                        me.did(act.activation(prob[:, i % 2, c, 0:kend], src[:, 0:kend], ACT.Exp, bias=red[:, i % 8, 2 + c:3 + c],
                                              scale=HD ** -0.5, accum_out=red[:, i % 8, 4 + c:5 + c]), sem["probs_ready"])
                if 0 <= i - 1 < len(units):
                    b, hh = units[i - 1]
                    src = bank.filled(act, "aT", i - 1)
                    if i - 1 >= 2:
                        act.wait_ge(sem["pe_tile"], bank.index[("o", i - 3)] + 1)
                    me.did(act.copy(attnT[:, (i - 1) % 2, 0:b + 1, :], src[:, 0:(b + 1) * P].rearrange("p (k q) -> p k q", q=P)),
                           sem["attnT_ready"])
                if 0 <= i - 2:
                    b, hh = units[i - 2]
                    src = bank.filled(act, "o", i - 2)
                    me.did(act.copy(qn[:, b, 0, hh * P:(hh + 1) * P], src[:, 0:P]), sem["o_ready"])
            act.wait_ge(sem["fin_ms"], 1)
            me.did(act.activation(rootq[:, 0:24], msq[:, 0:24], ACT.Sqrt), sem["fin_root"])
            for c in range(DC):
                src = bank.filled(act, "yT", c)
                me.did(act.copy(nT_hi[:, c, :], src), sem["high_ready"])

        @block.vector
        def _(dve):
            me = Line(dve, sem["dve_line"])

            def step(ins, s=None):
                me.did(ins, s)
                me.settle()

            for t in range(TB // 2, TB):
                dve.wait_ge(x_loaded[t], 16)
                me.did(dve.tensor_tensor_reduce(mix[:, t, :], x_in[:, t, :], x_in[:, t, :], 1.0, 0.0, ALU.mult, ALU.add, col(ss, t)), sem["sumsq_ready"])
            dve.wait_ge(sem["sumsq_ready"], TB)
            step(dve.tensor_scalar(ms, ss, 1.0 / D, EPS, ALU.mult, ALU.add), sem["ms_ready"])
            dve.wait_ge(sem["root_ready"], 1)
            step(dve.reciprocal(rstd, root))
            dve.wait_ge(x_loaded[0], 16)
            dve.wait_ge(x_loaded[1], 16)
            for t in range(TB):
                me.did(dve.tensor_scalar(mix[:, t, :], x_in[:, t, :], col(rstd, t), None, ALU.mult), sem["xn_ready"])
            dve.wait_ge(sem["const_loaded"], 64)
            for c in range(DC):
                dve.wait_ge(sem["high_ready"], c + 1)
                me.did(dve.scalar_tensor_tensor(nT_lo[:, c, :], bank.at("xT", c), col(cols, C_MIX + c), nT_hi[:, c, :].bitcast(F32), ALU.mult, ALU.subtract),
                       sem["nT_ready"])
            step(dve.tensor_copy(posf[:, :], posi[:, :]))
            A0, A1, A2 = (ang[:, i, :, :] for i in range(3))
            inv = con[:, K_INV:K_INV + 32].unsqueeze(1).to_broadcast([P, TB, 32])
            step(dve.tensor_tensor(A0, inv, spread_last(posf[:, :], 32), ALU.mult))
            step(dve.tensor_scalar(A1, A0, INV_2PI, None, ALU.mult))
            step(dve.tensor_scalar(A2, A1, MAGIC, None, ALU.add))
            step(dve.tensor_scalar(A1, A2, MAGIC, None, ALU.subtract))
            for part in (PI2_A, PI2_B, PI2_C):
                step(dve.scalar_tensor_tensor(A0, A1, -part, A0, ALU.mult, ALU.add))
            step(dve.tensor_scalar(A0, A0, float(np.float32(3.1415925)), -float(np.float32(3.1415925)), ALU.min, ALU.max), sem["sine_asked"])
            dve.wait_ge(sem["sine_ready"], 2)
            step(dve.tensor_tensor(A1, ang[:, 3, :, :], ang[:, 3, :, :], ALU.mult))
            step(dve.tensor_scalar(A1, A1, -2.0, 1.0, ALU.mult, ALU.add))
            for w, g0 in ((0, R_QG), (1, R_KG)):
                for half in range(2):
                    g_own = rows[:, g0 + 32 * half:g0 + 32 * half + 32].unsqueeze(1).to_broadcast([P, TB, 32])
                    g_other = rows[:, g0 + 32 * (1 - half):g0 + 32 * (1 - half) + 32].unsqueeze(1).to_broadcast([P, TB, 32])
                    me.did(dve.tensor_tensor(tab[:, 2 * w, :, half, :], A1, g_own, ALU.mult))
                    me.did(dve.scalar_tensor_tensor(tab[:, 2 * w + 1, :, half, :], ang[:, 4, :, :], 1.0 if half else -1.0, g_other,
                                                    ALU.mult, ALU.mult))
            for j in range(2):
                a0 = R_LAM + 128 * j
                me.did(dve.tensor_tensor_reduce(ropeA[:, 0, 64 * j:64 * j + 64], rows[:, a0:a0 + 64], rows[:, a0 + 64:a0 + 128], 1.0, 0.0,
                                                ALU.mult, ALU.add, col(lam, j)), None if j == 0 else sem["lam_asked"])
            me.settle()
            for c in range(XBC_C):
                src = bank.filled(dve, "xbc", c)
                tap = lambda k: col(cols, C_CW + TAPS * c + k)
                step(dve.tensor_scalar(xbcT[:, c, :], src, tap(3), col(cols, C_CB + c), ALU.mult, ALU.add))
                for k in (2, 1, 0):
                    s = 3 - k
                    step(dve.scalar_tensor_tensor(xbcT[:, c, s:T], src[:, 0:T - s], tap(k), xbcT[:, c, s:T], ALU.mult, ALU.add),
                         sem["conv_done"] if k == 0 else None)
            DT = lambda i: dts[:, i, :, :]
            src = bank.filled(dve, "dt", 0)
            bias = rows[:, R_DTB:R_DTB + 8].unsqueeze(1).to_broadcast([P, TB, 8])
            step(dve.tensor_tensor(DT(X_DT), src[:, 0:32].rearrange("p (t n) -> p t n", t=TB), bias, ALU.add), sem["dtraw_done"])
            step(dve.scalar_tensor_tensor(DT(X_A), DT(X_DT), -1.0, DT(X_DT), ALU.mult, ALU.max), sem["abs_ready"])
            dve.wait_ge(sem["edt_ready"], 1)
            step(dve.tensor_scalar(DT(X_A), DT(X_B), 2.0, None, ALU.add))
            step(dve.reciprocal(DT(X_C), DT(X_A)))
            step(dve.tensor_tensor(DT(X_A), DT(X_B), DT(X_C), ALU.mult))
            step(dve.tensor_tensor(DT(X_B), DT(X_A), DT(X_A), ALU.mult))
            step(dve.tensor_scalar(DT(X_C), DT(X_B), 2.0 / 17, 2.0 / 15, ALU.mult, ALU.add))
            for n in (13, 11, 9, 7, 5, 3, 1):
                step(dve.tensor_tensor(DT(X_C), DT(X_C), DT(X_B), ALU.mult))
                step(dve.tensor_scalar(DT(X_C), DT(X_C), 2.0 / n, None, ALU.add))
            step(dve.tensor_tensor(DT(X_C), DT(X_C), DT(X_A), ALU.mult))
            step(dve.scalar_tensor_tensor(DT(X_DT), DT(X_DT), 0.0, DT(X_C), ALU.max, ALU.add))
            dve.wait_ge(sem["aexp_ready"], 1)
            step(dve.scalar_tensor_tensor(DT(X_DA), DT(X_DT), -1.0, a_rate.unsqueeze(1).to_broadcast([P, TB, 8]), ALU.mult, ALU.mult),
                 sem["dt_asked"])
            dve.wait_ge(sem["lam_exp"], 1)
            step(dve.tensor_tensor(lam[:, 4:5], lam[:, 3:4], lam[:, 2:3], ALU.subtract))
            step(dve.tensor_scalar(lam[:, 5:6], lam[:, 4:5], LAM_INIT, None, ALU.subtract))
            for i in range(4 * TB):
                w, half, t = i // (2 * TB), i // TB % 2, i % TB
                src = bank.filled(dve, "qk"[w], half * TB + t)[:, 0:256]
                dve.wait_ge(sem["qksq_ready"], i + 1)
                step(dve.tensor_reduce(qks[:, 2, i, :], sqj[:, 0:256].rearrange("p (h d) -> p h d", d=HD), AX.X, ALU.add))
                me.did(dve.tensor_scalar(qks[:, 0, i, :], qks[:, 2, i, :], 1.0 / HD, EPS, ALU.mult, ALU.add), sem["qkms_ready"])
                two = lambda ap: ap.rearrange("p (h two r) -> p h two r", two=2, r=32)
                ra, rb = ropeA[:, i % 2, 0:256], ropeB[:, i % 2, 0:256]
                q4, a4, b4 = two(src), two(ra), two(rb)
                cosg = tab[:, 2 * w, t, :, :].unsqueeze(1).to_broadcast([P, 4, 2, 32])
                me.did(dve.tensor_tensor(a4, q4, cosg, ALU.mult))
                for side in range(2):
                    sing = tab[:, 2 * w + 1, t, side, :].unsqueeze(1).to_broadcast([P, 4, 32])
                    me.did(dve.tensor_tensor(b4[:, :, side, :], q4[:, :, 1 - side, :], sing, ALU.mult))
                me.settle()
                step(dve.tensor_tensor(ra, ra, rb, ALU.add), sem["qk_roped"])
                dve.wait_ge(sem["qkroot_ready"], i + 1)
                step(dve.reciprocal(qks[:, 3, i, :], qks[:, 1, i, :]))
                step(dve.tensor_tensor(qn[:, t, w, half * 256:(half + 1) * 256].rearrange("p (h d) -> p h d", d=HD),
                                       ra.rearrange("p (h d) -> p h d", d=HD), spread_last(qks[:, 3, i, :], HD), ALU.mult), sem["qk_ready"])
            h8 = lambda ap: ap.rearrange("p (h d) -> p h d", d=HD)
            for t in range(TB):
                src = bank.filled(dve, "cs", t)
                step(dve.tensor_scalar(dts[:, X_NCS, t, :], src[:, 0:SSD_H], -1.0, None, ALU.mult), sem["ncs_ready"])
                dve.wait_ge(sem["xs_ready"], t + 1)
                if t:
                    dve.wait_ge(sem["pe_tile"], bank.index[("st", t - 1)] + 1)
                step(dve.tensor_tensor(h8(xdt[:, :]), h8(xs[:, t, :]), spread_last(dts[:, X_DT, t, :], HD), ALU.mult), sem["xdt_ready"])
                dve.wait_ge(sem["decay_ready"], 2 * t + 2)
                dl = spread_last(dec[:, :, :, :].rearrange("p g r l -> p (g r) l")[:, :, P - 1], HD)
                me.did(dve.tensor_tensor(h8(xdtd[:, :]), h8(xdt[:, :]), dl, ALU.mult), sem["xdt_ready"])
                cb = bank.filled(dve, "cb", t)
                for g in range(SSD_G):
                    me.did(dve.tensor_tensor(Mt[:, g * HPG:(g + 1) * HPG, :], dec[:, g, :, :],
                                             cb[:, g * P:(g + 1) * P].unsqueeze(1).to_broadcast([P, HPG, P]), ALU.mult), sem["m_ready"])
                ym = mix[:, t, 0:SSD_W]
                if t == 0:
                    dve.wait_ge(sem["pe_tile"], bank.index[("xT", DC - 1)] + 1)
                step(dve.tensor_tensor(h8(ym), h8(xs[:, t, :]), spread_last(rows[:, R_DSK:R_DSK + 8], HD), ALU.mult))
                if t:
                    src = bank.filled(dve, "yo", t)
                    dve.wait_ge(sem["ecs_ready"], t + 1)
                    step(dve.tensor_tensor(h8(ropeA[:, 0, :]), h8(src), spread_last(dts[:, X_ECS, t, :], HD), ALU.mult))
                    step(dve.tensor_tensor(ym, ym, ropeA[:, 0, :], ALU.add))
                src = bank.filled(dve, "y", t)
                step(dve.tensor_tensor(ym, ym, src, ALU.add), sem["y_ready"])
                if t < TB - 1:
                    src = bank.filled(dve, "st", t)
                    if t == 0:
                        step(dve.tensor_copy(state[:, :], src), sem["state_ready"])
                    else:
                        step(dve.tensor_tensor(h8(state[:, :]), h8(state[:, :]), spread_last(ecl[:, :], HD), ALU.mult))
                        step(dve.tensor_tensor(state[:, :], state[:, :], src, ALU.add), sem["state_ready"])

            def gate_scan(t):
                ym = mix[:, t, 0:SSD_W]
                dve.wait_ge(sem["z_ready"], t + 1)
                step(dve.tensor_tensor(ym, ym, zs[:, t, :], ALU.mult))
                for g in range(SSD_G):
                    yg = ym[:, g * 256:(g + 1) * 256]
                    me.did(dve.tensor_tensor_reduce(ropeB[:, 0, g * 256:(g + 1) * 256], yg, yg, 1.0, 0.0, ALU.mult, ALU.add, col(ssq, 2 * t + g)))
                me.settle()

            for i, (b, hh) in enumerate(units):
                kend = (b + 1) * P
                rd = red[:, i % 8, :]
                for c in range(2):
                    src = bank.filled(dve, "s", i, c)
                    step(dve.tensor_reduce(rd[:, c:c + 1], src[:, 0:kend], AX.X, ALU.max, negate=True))
                    step(dve.tensor_scalar(rd[:, 2 + c:3 + c], rd[:, c:c + 1], HD ** -0.5, None, ALU.mult), sem["bias_ready"])
                dve.wait_ge(sem["probs_ready"], 2 * i + 2)
                step(dve.reciprocal(rd[:, 6:8], rd[:, 4:6]))
                step(dve.tensor_tensor(rd[:, 7:8], rd[:, 7:8], lam[:, 5:6], ALU.mult))
                if i >= 2:
                    dve.wait_ge(sem["pe_tile"], bank.index[("aT", i - 2)] + 1)
                step(dve.tensor_scalar(attn[:, i % 2, 0:kend], prob[:, i % 2, 0, 0:kend], rd[:, 6:7], None, ALU.mult))
                step(dve.scalar_tensor_tensor(attn[:, i % 2, 0:kend], prob[:, i % 2, 1, 0:kend], rd[:, 7:8], attn[:, i % 2, 0:kend],
                                              ALU.mult, ALU.add), sem["attn_ready"])
                if 1 <= i <= TB:
                    gate_scan(i - 1)
            for b in range(TB):
                dve.wait_ge(sem["o_ready"], DIFF_H * (b + 1))
                for hh in range(DIFF_H):
                    o = qn[:, b, 0, hh * P:(hh + 1) * P]
                    me.did(dve.tensor_tensor_reduce(ropeA[:, b % 2, hh * P:(hh + 1) * P], o, o, 1.0, 0.0, ALU.mult, ALU.add,
                                                    col(ssq, 8 + 4 * b + hh)))
                me.settle()
            me.did(dve.tensor_scalar(msq[:, 0:8], ssq[:, 0:8], SSD_G / SSD_W, EPS, ALU.mult, ALU.add))
            step(dve.tensor_scalar(msq[:, 8:24], ssq[:, 8:24], 1.0 / P, EPS, ALU.mult, ALU.add), sem["fin_ms"])
            dve.wait_ge(sem["fin_root"], 1)
            step(dve.reciprocal(rstdq[:, 0:24], rootq[:, 0:24]))
            step(dve.tensor_scalar(rstdq[:, 8:24], rstdq[:, 8:24], 1.0 - LAM_INIT, None, ALU.mult))
            for t in range(TB):
                for g in range(SSD_G):
                    yg = mix[:, t, g * 256:(g + 1) * 256]
                    me.did(dve.scalar_tensor_tensor(yg, yg, col(rstdq, 2 * t + g), rows[:, R_SG + 256 * g:R_SG + 256 * g + 256], ALU.mult, ALU.mult),
                           sem["mix_ready"] if g else None)
                for hh in range(DIFF_H):
                    me.did(dve.scalar_tensor_tensor(mix[:, t, SSD_W + hh * P:SSD_W + (hh + 1) * P], qn[:, t, 0, hh * P:(hh + 1) * P],
                                                    col(rstdq, 8 + 4 * t + hh), rows[:, R_DG:R_DG + P], ALU.mult, ALU.mult),
                           sem["mix_ready"] if hh == DIFF_H - 1 else None)
            for c in range(DC):
                dve.wait_ge(sem["high_ready"], DC + c + 1)
                me.did(dve.tensor_tensor(nT_lo[:, c, :], bank.at("yT", c), nT_hi[:, c, :].bitcast(F32), ALU.subtract), sem["nT_ready"])
            dve.wait_ge(sem["x_again"], 16 * TB)
            for n in range(4):
                for t in range(TB):
                    src = bank.filled(dve, "h", n * TB + t)[:, 0:256]
                    hv = h[:, t, n * 256:(n + 1) * 256]
                    me.did(dve.tensor_tensor(hv, hv, src, ALU.add), sem["h_ready"])
    new_sem.free()


def retrieval(nc, shared, io, h_dram):
    h, con, cols, hn_hi, hn_lo, scores = (shared[k] for k in ("h", "con", "cols", "hn_hi", "hn_lo", "scores"))
    new_sem = Semaphores(nc)
    with ExitStack() as ctx:
        sb = lambda n, s, d=F32: ctx.enter_context(nc.sbuf_tensor(n, s, d))
        names = ["sumsq_ready", "ms_ready", "root_ready", "xn_ready", "high_ready", "nT_ready", "qT_ready", "scores_ready",
                 "k_loaded", "gain_loaded", "h_stored", "row_ready", "pe_tile", "act_line", "dve_line"]
        sem = {n: new_sem("r_" + n) for n in names}
        psum = ctx.enter_context(nc.psum_tensor("r_psum", [P, 8, 512], F32))
        tiles = [(("nT", c), "nT_ready", c + 1) for c in range(DC)]
        tiles += [(("q", f), "qT_ready", f + 1) for f in range(LISTS)]
        tiles += [(("s", i), "scores_ready", i + 1) for i in range(TB * LISTS // 4)]
        bank = Banks(psum, tiles, sem, sem["pe_tile"])
        weights = Weights(sb, new_sem, "r", LISTS // 2)
        keys = sb("r_keys", [P, 2, NK])
        qx = sb("r_qx", [P, LISTS, T])
        gain = sb("r_gain", [P, D])
        hn = (hn_hi, hn_lo)
        small = sb("r_small", [P, 16])
        ss, ms, root, rstd = (small[:, 4 * i:4 * i + 4] for i in range(4))
        ident = con[:, K_ID:K_ID + P]
        xn = lambda t: qx[:, 2 * t:2 * t + 2, :].rearrange("p a n -> p (a n)")
        block = ctx.enter_context(nc.Block())

        @block.sync
        def _(sp):
            sp.dma_start(keys[:, :, :], io["keys"].rearrange("p (a k) -> p a k", a=2)).then_inc(sem["k_loaded"], 16)
            sp.dma_start(gain[:, :], io["ffn_gain"]).then_inc(sem["gain_loaded"], 16)
            for t in range(TB):
                sp.dma_start(h_dram[t], h[:, t, :]).then_inc(sem["h_stored"], 16)
            for n in range(LISTS // 2):
                weights.load(sp, n, io["w_q"][n])
            sp.wait_ge(sem["h_stored"], 16 * TB)

        @block.gpsimd
        def _(pool):
            weights.cut(pool)

        @block.tensor
        def _(pe):
            turn_blocks(pe, bank, "nT", sem["xn_ready"], 1, lambda t, c: xn(t)[:, c * P:(c + 1) * P], ident)
            for f in range(LISTS):
                w = weights.ready(pe, f // 2)
                out = bank.take(pe, "q", f)
                last = product(pe, out, lambda part, d: w[part][:, d, (f % 2) * P:(f % 2 + 1) * P], lambda part, d: hn[part][:, d, :],
                               made=(sem["nT_ready"], 0) if f == 0 else None)
                last.then_inc(sem["pe_tile"], 1)
                if f % 2:
                    pe.drain().then_inc(weights.used[f // 2 % 2], 1)
            pe.wait_ge(sem["k_loaded"], 16)
            pe.wait_ge(sem["qT_ready"], LISTS)
            for i in range(TB * LISTS // 4):
                t, f0 = i // 4, (i % 4) * 4
                out = bank.take(pe, "s", i)
                for j in range(4):
                    last = pe.matmul(out[:, j * NK:(j + 1) * NK], qx[:, f0 + j, t * P:(t + 1) * P], keys[:, j % 2, :], start=True, stop=True)
                last.then_inc(sem["pe_tile"], 1)

        @block.scalar
        def _(act):
            me = Line(act, sem["act_line"])
            for t in range(TB // 2):
                me.did(act.activation(xn(t), h[:, t, :], ACT.Square, accum_out=col(ss, t)), sem["sumsq_ready"])
            act.wait_ge(sem["ms_ready"], 1)
            me.did(act.activation(root, ms, ACT.Sqrt), sem["root_ready"])
            for c in range(DC):
                src = bank.filled(act, "nT", c)
                me.did(act.activation(hn_hi[:, c, :], src, ACT.Copy, scale=col(cols, C_FFN + c)), sem["high_ready"])
            act.wait_ge(sem["row_ready"], 1)
            for f in range(LISTS):
                src = bank.filled(act, "q", f)
                me.did(act.copy(qx[:, f, :], src), sem["qT_ready"])

        @block.vector
        def _(dve):
            me = Line(dve, sem["dve_line"])
            for t in range(TB // 2, TB):
                me.did(dve.tensor_tensor_reduce(xn(t), h[:, t, :], h[:, t, :], 1.0, 0.0, ALU.mult, ALU.add, col(ss, t)), sem["sumsq_ready"])
            dve.wait_ge(sem["sumsq_ready"], TB)
            me.did(dve.tensor_scalar(ms, ss, 1.0 / D, EPS, ALU.mult, ALU.add), sem["ms_ready"])
            dve.wait_ge(sem["root_ready"], 1)
            me.did(dve.reciprocal(rstd, root))
            me.settle()
            for t in range(TB):
                me.did(dve.tensor_scalar(xn(t), h[:, t, :], col(rstd, t), None, ALU.mult), sem["xn_ready"])
            for c in range(DC):
                dve.wait_ge(sem["high_ready"], c + 1)
                me.did(dve.scalar_tensor_tensor(hn_lo[:, c, :], bank.at("nT", c), col(cols, C_FFN + c), hn_hi[:, c, :].bitcast(F32), ALU.mult, ALU.subtract),
                       sem["nT_ready"])
            dve.wait_ge(sem["gain_loaded"], 16)
            dve.wait_ge(sem["h_stored"], 16 * TB)
            me.settle()
            me.did(dve.tensor_tensor(h[:, TB - 1, :], xn(0), gain[:, :], ALU.mult), sem["row_ready"])
            for i in range(TB * LISTS // 4):
                src = bank.filled(dve, "s", i)
                me.did(dve.tensor_copy(scores[:, i // 4, (i % 4) * 4:(i % 4) * 4 + 4, :], src.rearrange("p (l k) -> p l k", k=NK)),
                       sem["scores_ready"])
    new_sem.free()


def experts(nc, shared, io, act_dram, gate_dram, h_dram):
    con, hn_hi, hn_lo, scores, h = (shared[k] for k in ("con", "hn_hi", "hn_lo", "scores", "h"))
    hn_row = h[:, TB - 1, :]
    WAITS = 25
    OPS = 1 + 5 * LISTS + 2 + 2 * (LONG_ROWS + 1) + 5 * PH + 2 + 6 + 4 + WAITS
    n_steps = NK
    turns = n_steps // UR
    n_body = DT // (8 * STEP_TOK)
    LOOP_C = LOOP_A + 8 * n_body
    OUTS = 2 * (TB - 1)
    new_sem = Semaphores(nc)
    with ExitStack() as ctx:
        sb = lambda n, s, d=F32: ctx.enter_context(nc.sbuf_tensor(n, s, d))
        S = lambda n: new_sem("s_" + n)
        ring = lambda n, k: [S(f"{n}{i}") for i in range(k)]
        tile_loaded, hi_ready, lo_ready, tile_used, act_ready, act_stored = (
            ring(n, UR) for n in ("tile_loaded", "hi_ready", "lo_ready", "tile_used", "act_ready", "act_stored"))
        spread_ready, gates_summed, gates_copied = (ring(n, 2) for n in ("spread_ready", "gates_summed", "gates_copied"))
        gates_stored = ring("gates_stored", 2)
        row_loaded, dotted = ring("row_loaded", U_RING), ring("dotted", U_RING)
        rows_known, dots_ready, w0_gelu = S("rows_known"), S("dots_ready"), S("w0_gelu")
        dve_line, act_line = S("dve_line"), S("act_line")
        exp_ready, found_ready, turned, turned_copied = (
            S(n) for n in ("exp_ready", "found_ready", "turned", "turned_copied"))
        in_loaded, wg_ready, whi_ready, wlo_ready = (ring(n, 2) for n in ("in_loaded", "wg_ready", "whi_ready", "wlo_ready"))
        vrow_loaded, vrow_added = ring("vrow_loaded", UR), ring("vrow_added", UR)
        h0_loaded, h_loaded, h_added = S("h0_loaded"), S("h_loaded"), S("h_added")
        psU = ctx.enter_context(nc.psum_tensor("s_psU", [P, UR, 512], F32))
        psG = ctx.enter_context(nc.psum_tensor("s_psG", [P, 2, 2, 4, P], F32))
        outs = [psG[:, o // 2, o % 2, :, :].rearrange("p a b -> p (a b)") for o in range(4)] + [psU[:, o, :] for o in range(OUTS - 4)]

        more_rows = sb("s_more_rows", [P, U_RING - (TB - 1), D])
        rows = [h[:, s, :] for s in range(TB - 1)] + [more_rows[:, s, :] for s in range(U_RING - (TB - 1))]
        raw = sb("s_raw", [P, UR, D])
        hi = sb("s_hi", [P, UR, D], F32R)
        lo = sb("s_lo", [P, UR, D], F32R)
        acts = sb("s_acts", [P, UR, DT])
        w_hi = sb("s_whi", [P, 2, UR, DT], F32R)
        w_lo = sb("s_wlo", [P, 2, UR, DT], F32R)
        gtile = sb("s_gtile", [P, 2, NK, GT])
        work = gtile[:, :, :, :].rearrange("p a i t -> p a (i t)")
        match = work[:, 0, 0:4 * TOPK * CAND].rearrange("p (h k c) -> p h k c", h=4, k=TOPK)
        after_match = work[:, 0, 4 * TOPK * CAND:]
        top, posf = (after_match[:, i * PAIRS:(i + 1) * PAIRS].rearrange("p (h k) -> p h k", h=PH) for i in range(2))
        idi = after_match[:, 2 * PAIRS:5 * PAIRS].rearrange("p (j n) -> p j n", j=3).bitcast(I32)
        cut = {}
        at = 0
        for name, n in (("s_cur", LISTS * NK), ("best", LISTS * TOPK), ("bestf", LISTS * TOPK), ("cand", 2 * PH * CAND), ("cid", PH * CAND)):
            cut[name] = work[:, 1, at:at + n]
            at += n
        assert at <= NK * GT and 4 * TOPK * CAND + 5 * PAIRS <= NK * GT
        s_cur = cut["s_cur"].rearrange("p (l k) -> p l k", l=LISTS)
        best, bestf = (cut[n].rearrange("p (l k) -> p l k", l=LISTS) for n in ("best", "bestf"))
        cand = cut["cand"].rearrange("p (a h c) -> p a h c", a=2, h=PH)
        cid = cut["cid"].rearrange("p (h c) -> p h c", h=PH)
        vrows = work[:, 0, :].rearrange("p (k d) -> p k d", k=UR)
        flat = scores[:, :, :, :].rearrange("p t l k -> p (t l k)")
        n_hot = 4 * STEP_TOK * P
        onehot = flat[:, 0:n_hot].rearrange("p (a b n k) -> p a b n k", a=2, b=2, k=P)
        pair = flat[:, n_hot:n_hot + 3 * DT].rearrange("p (j t) -> p j t", j=3)
        a_in = flat[:, 0:2 * UR * DT].rearrange("p (a i t) -> p a i t", a=2, i=UR)
        g_in = flat[:, 2 * UR * DT:4 * UR * DT].rearrange("p (a g i t) -> p a g i t", a=2, i=UR, t=GT)
        hold = sb("s_hold", [P, 1])
        u_row = sb("s_u_row", [P, PAIRS], U32)
        v_row = sb("s_v_row", [P, PAIRS], U32)
        w0 = sb("s_w0", [P, PAIRS])
        dots = sb("s_dots", [P, PAIRS])
        dot_slot = sb("s_dot_slot", [P, 24])
        besti = sb("s_besti", [P, LISTS, TOPK], U32)
        pos = sb("s_pos", [P, PH, TOPK], U32)
        found = sb("s_found", [P, TB, 3, PAIRS])
        zsum = sb("s_zsum", [P, 2, TB * PH])
        v_rows = io["v_t"].rearrange("i p d -> (i p) d")
        ident, iota = con[:, K_ID:K_ID + P], con[:, K_IOTA:K_IOTA + P]

        block = ctx.enter_context(nc.Block())

        @block.sync
        def _(sp):
            def store_acts(step, s, turn):
                sp.wait_ge(act_ready[s], turn)
                sp.dma_start(act_dram[step], acts[:, s, :]).then_inc(act_stored[s], 16)

            def load_values(g):
                for s in range(UR):
                    sp.wait_ge(lo_ready[s], g + turns)
                    sp.dma_start(raw[:, s, :], io["v_t"][g * UR + s]).then_inc(tile_loaded[s], 16)
                    if isinstance(g, int) and g == 0:
                        store_acts(n_steps - UR + s, s, turns)

            def load_weights(g, par, used):
                reached(sp, wlo_ready[par], used)
                sp.dma_start(a_in[:, par, :, :], act_dram[bass.ds(g * UR, UR)].rearrange("i p t -> p i t")).then_inc(in_loaded[par], 16)
                sp.dma_start(g_in[:, par, :, :, :], gate_dram[:, :, bass.ds(g * UR, UR), :].rearrange("g p i t -> p g i t")).then_inc(in_loaded[par], 16)

            for s in range(UR):
                sp.dma_start(raw[:, s, :], io["u_t"][s]).then_inc(tile_loaded[s], 16)
            with sp.Fori(1, turns) as it:
                for s in range(UR):
                    sp.wait_ge(lo_ready[s], it)
                    sp.dma_start(raw[:, s, :], io["u_t"][it * UR + s]).then_inc(tile_loaded[s], 16)
                    store_acts(it * UR + (s - UR), s, it)
            for tile in range(2):
                sp.wait_ge(gates_stored[tile], 16 * n_body)
            for s in range(UR):
                sp.wait_ge(act_stored[s], 16 * 2)
            load_weights(0, 0, 0)
            load_weights(1, 1, 0)
            load_values(0)
            for s in range(UR):
                sp.wait_ge(act_stored[s], 16 * turns)
            sp.wait_ge(dots_ready, 1)
            sp.dma_start(h[:, 0, :], h_dram[0]).then_inc(h0_loaded, 16)
            load_values(1)
            for t in range(1, TB):
                sp.dma_start(h[:, t, :], h_dram[t]).then_inc(h_loaded, 16)
            with sp.Fori(1, turns // 2) as i:
                load_weights(2 * i, 0, i)
                load_values(2 * i)
                load_weights(2 * i + 1, 1, i)
                load_values(2 * i + 1)

        @block.gpsimd
        def _(pool):
            pair_no = 0

            def low_part(n):
                s, it = n % UR, n // UR
                pool.wait_ge(hi_ready[s], it + 1)
                reached(pool, tile_used[s], it)
                pool.tensor_tensor(lo[:, s, :], raw[:, s, :], hi[:, s, :].bitcast(F32), ALU.subtract).then_inc(lo_ready[s], 1)

            def gather():
                nonlocal pair_no
                c, s = pair_no, pair_no % U_RING
                if c == 0:
                    pool.wait_ge(rows_known, 2)
                reached(pool, dotted[s], c // U_RING)
                pool.indirect_dma_start(rows[s], None, io["u_rows"], bass.IndirectOffsetOnAxis(ap=u_row[:, c:c + 1], axis=0),
                                        bounds_check=NK * NK - 1).then_inc(row_loaded[s], 16)
                pair_no += 1

            def due(n):
                in_a, in_b = DOTS_1 + (TB - 1) * DOTS_T, DOTS_J * n_body
                for start, end, before, count in ((FIRST_GATHER, EXP_AT, 0, in_a), (LOOP_A, LOOP_C, in_a, in_b),
                                                  (LOOP_C, n_steps, in_a + in_b, PAIRS - in_a - in_b)):
                    if n < end:
                        return before + max(0, min(count, (n - start + 3) * count // (end - start)))

            for n in range(n_steps):
                low_part(n)
                while pair_no < due(n):
                    gather()
            assert pair_no == PAIRS
            for n in range(n_steps):
                low_part(n_steps + n)
                k, g = n % UR, n // UR
                if n == 0:
                    for tile in range(2):
                        pool.wait_ge(gates_stored[tile], 16 * n_body)
                reached(pool, vrow_added[k], g)
                pool.indirect_dma_start(vrows[:, k, :], None, v_rows, bass.IndirectOffsetOnAxis(ap=v_row[:, n:n + 1], axis=0),
                                        bounds_check=NK * NK - 1).then_inc(vrow_loaded[k], 16)

        @block.tensor
        def _(pe):
            def score(it, s):
                pe.wait_ge(lo_ready[s], it + 1)
                reached(pe, act_ready[s], it)
                for d in range(DC):
                    for n, (uu, hh) in enumerate(((hi, hn_hi), (hi, hn_lo), (lo, hn_hi))):
                        last = pe.matmul(psU[:, s, 0:DT], uu[:, s, d * P:(d + 1) * P], hh[:, d, P:T],
                                         start=(n == 0 and d == 0), stop=(n == 2 and d == DC - 1))
                last.then_inc(tile_used[s], 1)

            for s in range(UR):
                score(0, s)
            with pe.Fori(1, TURN_AT // UR) as it:
                for s in range(UR):
                    score(it, s)
            pe.wait_ge(found_ready, 1)
            for j in range(3):
                for t in range(1, TB):
                    last = pe.transpose(psG[:, j // 2, j % 2, t - 1, :], found[:, t, j, :], ident)
            last.then_inc(turned, 1)
            with pe.Fori(TURN_AT // UR, LOOP_A // UR) as it:
                for s in range(UR):
                    score(it, s)

            def spread_and_score(j):
                for k in range(8):
                    par = k % 2
                    pe.wait_ge(spread_ready[par], 4 * j + k // 2 + 1)
                    reached(pe, gates_copied[par], 4 * j + k // 2)
                    for n in range(STEP_TOK):
                        last = pe.matmul(psG[:, par, n // 4, n % 4, :], onehot[:, par, 0, n, :], onehot[:, par, 1, n, :],
                                         start=True, stop=True)
                    last.then_inc(gates_summed[par], 1)
                    score(2 * j + (LOOP_A // UR + k // UR), k % UR)

            spread_and_score(0)
            with pe.Fori(1, n_body) as j:
                spread_and_score(j)
            with pe.Fori(LOOP_C // UR, turns) as it:
                for s in range(UR):
                    score(it, s)

            def sum_values(g, par, turn, first=False, final=False):
                pe.wait_ge(wlo_ready[par], turn)
                for s in range(UR):
                    pe.wait_ge(lo_ready[s], g + (turns + 1))
                    for o in range(OUTS):
                        t, half = o // 2, o % 2
                        for m, (ww, vv) in enumerate(((w_hi, hi), (w_hi, lo), (w_lo, hi))):
                            last = pe.matmul(outs[o], ww[:, par, s, t * P:(t + 1) * P], vv[:, s, half * 512:(half + 1) * 512],
                                             start=(first and s == 0 and m == 0), stop=(final and s == UR - 1 and m == 2))
                    last.then_inc(tile_used[s], 1)

            for par in range(2):
                pe.wait_ge(gates_copied[par], 4 * n_body)
            for s in range(OUTS - 4):
                pe.wait_ge(act_ready[s], turns)
            sum_values(0, 0, 1, first=True)
            sum_values(1, 1, 1)
            with pe.Fori(1, turns // 2 - 1) as i:
                sum_values(2 * i, 0, i + 1)
                sum_values(2 * i + 1, 1, i + 1)
            sum_values(turns - 2, 0, turns // 2)
            sum_values(turns - 1, 1, turns // 2, final=True)

        @block.scalar
        def _(act):
            def split(it, s):
                act.wait_ge(tile_loaded[s], 16 * it + 16)
                reached(act, tile_used[s], it)
                reached(act, lo_ready[s], it)
                act.copy(hi[:, s, :], raw[:, s, :]).then_inc(hi_ready[s], 1)

            def gelu(it, s):
                act.wait_ge(tile_used[s], it + 1)
                reached(act, act_stored[s], 16 * it)
                act.activation(acts[:, s, :], psU[:, s, 0:DT], ACT.Gelu).then_inc(act_ready[s], 1)

            split(0, 0)
            split(0, 1)
            for s in range(UR):
                split((s + 2) // UR, (s + 2) % UR)
                gelu(0, s)
            with act.Fori(1, EXP_AT // UR) as it:
                for s in range(UR):
                    split(it + (s + 2) // UR, (s + 2) % UR)
                    gelu(it, s)
            act.wait_ge(dve_line, TB * OPS)
            act.activation(found[:, :, 2, :], found[:, :, 2, :], ACT.Exp).then_inc(exp_ready, 1)
            with act.Fori(EXP_AT // UR, LOOP_A // UR) as it:
                for s in range(UR):
                    split(it + (s + 2) // UR, (s + 2) % UR)
                    gelu(it, s)

            def steps(j):
                for k in range(8):
                    par, tile = k % 2, k // 4
                    split(2 * j + (LOOP_A // UR + (k + 2) // UR), (k + 2) % UR)
                    act.wait_ge(gates_summed[par], 4 * j + k // 2 + 1)
                    if k % 4 == 0:
                        reached(act, gates_stored[tile], 16 * j)
                    for half in range(2):
                        t0 = (k % 4) * STEP_TOK + half * 4
                        ins = act.copy(gtile[:, tile, :, t0:t0 + 4].rearrange("p i t -> p t i"), psG[:, par, half, :, :])
                        ins.then_inc(gates_copied[par] if half else act_line, 1)
                    gelu(2 * j + (LOOP_A // UR + k // UR), k % UR)
                    if k % 4 == 3:
                        act.wait_ge(gates_copied[1], 4 * j + k // 2 + 1)
                        act.dma_start(gate_dram[2 * j + tile], gtile[:, tile, :, :]).then_inc(gates_stored[tile], 16)

            steps(0)
            with act.Fori(1, n_body) as j:
                steps(j)
            with act.Fori(LOOP_C // UR, turns) as it:
                for s in range(UR):
                    split(it + (s + 2) // UR, (s + 2) % UR)
                    gelu(it, s)
            def high_weights(par, turn, used):
                reached(act, tile_used[UR - 1], used)
                act.wait_ge(wg_ready[par], turn)
                act.copy(w_hi[:, par, :, :], a_in[:, par, :, :]).then_inc(whi_ready[par], 1)

            def high_values(g, par, turn, final=False):
                split(g + turns, 2)
                split(g + turns, 3)
                if not final:
                    high_weights(par, turn, g + turns)
                    split(g + (turns + 1), 0)
                    split(g + (turns + 1), 1)

            high_weights(0, 1, 0)
            act.wait_ge(dots_ready, 1)
            act.activation(w0[:, :], dots[:, :], ACT.Gelu).then_inc(w0_gelu, 1)
            high_values(0, 1, 1)
            with act.Fori(1, turns // 2) as i:
                high_values(2 * i - 1, 0, i + 1)
                high_values(2 * i, 1, i + 1)
            high_values(turns - 1, 0, 0, final=True)

        @block.vector
        def _(dve):
            def dot(s, rounds, k):
                dve.wait_ge(row_loaded[s], 16 * rounds)
                dve.tensor_tensor_reduce(rows[s], rows[s], hn_row, 1.0, 0.0, ALU.mult, ALU.add, col(dot_slot, k))\
                    .then_inc(dotted[s], 1)

            def retrieve(t, n_dots):
                me = Line(dve, dve_line)
                did = me.did
                n_waits = 0

                def wait():
                    nonlocal n_waits
                    if n_dots and n_waits in DOT_AT:
                        k = DOT_AT.index(n_waits)
                        dot((DOTS_1 + k) % U_RING, DOTS_T // U_RING * (t - 1) + (DOTS_1 + k) // U_RING + 1, k)
                    n_waits += 1
                    dve.wait_ge(dve_line, me.count[id(dve_line)] + t * OPS)
                    did(dve.memset(hold[:, :], 0.0))

                did(dve.tensor_copy(s_cur[:, :, :], scores[:, t, :, :]))
                wait()
                for l in range(LISTS):
                    did(dve.max(best[:, l, 0:8], s_cur[:, l, :]))
                wait()
                for l in range(LISTS):
                    did(dve.max_index(besti[:, l, 0:8], best[:, l, 0:8], s_cur[:, l, :]))
                wait()
                for l in range(LISTS):
                    did(dve.match_replace(s_cur[:, l, :], best[:, l, 0:8], s_cur[:, l, :], LOWEST))
                wait()
                for l in range(LISTS):
                    did(dve.max(best[:, l, 8:16], s_cur[:, l, :]))
                wait()
                for l in range(LISTS):
                    did(dve.max_index(besti[:, l, 8:16], best[:, l, 8:16], s_cur[:, l, :]))
                wait()
                did(dve.tensor_copy(bestf[:, :, :], besti[:, :, :]))
                wait()
                b4 = best[:, :, :].rearrange("p (h two) k -> p h two k", two=2)
                i4 = bestf[:, :, :].rearrange("p (h two) k -> p h two k", two=2)
                did(dve.tensor_scalar(i4[:, :, 0, :], i4[:, :, 0, :], float(NK), None, ALU.mult))
                wait()
                for out, src in ((cand[:, 0, :, :], b4), (cid, i4)):
                    at = 0
                    for i in range(LONG_ROWS):
                        n = ROW_LEN[i]
                        did(dve.tensor_tensor(out[:, :, at:at + n], src[:, :, 1, 0:n], src[:, :, 0, i:i + 1].to_broadcast([P, PH, n]), ALU.add))
                        at += n
                    did(dve.tensor_tensor(out[:, :, at:CAND], src[:, :, 0, LONG_ROWS:TOPK],
                                          src[:, :, 1, 0:1].to_broadcast([P, PH, TOPK - LONG_ROWS]), ALU.add))
                wait()
                for hh in range(PH):
                    did(dve.max(top[:, hh, 0:8], cand[:, 0, hh, :]))
                wait()
                for hh in range(PH):
                    did(dve.max_index(pos[:, hh, 0:8], top[:, hh, 0:8], cand[:, 0, hh, :]))
                for hh in range(PH):
                    did(dve.match_replace(cand[:, 1, hh, :], top[:, hh, 0:8], cand[:, 0, hh, :], LOWEST))
                wait()
                for hh in range(PH):
                    did(dve.max(top[:, hh, 8:16], cand[:, 1, hh, :]))
                wait()
                for hh in range(PH):
                    did(dve.max_index(pos[:, hh, 8:16], top[:, hh, 8:16], cand[:, 1, hh, :]))
                wait()
                did(dve.tensor_copy(posf[:, :, :], pos[:, :, :]))
                did(dve.tensor_tensor(found[:, t, 2, :].rearrange("p (h k) -> p h k", h=PH), top[:, :, :],
                                      top[:, :, 0:1].to_broadcast([P, PH, TOPK]), ALU.subtract))
                wait()
                for half in range(2):
                    hs = slice(4 * half, 4 * half + 4)
                    io50 = iota[:, 0:CAND].unsqueeze(1).unsqueeze(1).to_broadcast([P, 4, TOPK, CAND])
                    did(dve.tensor_tensor(match, io50, spread_last(posf[:, hs, :], CAND), ALU.is_equal))
                    wait()
                    did(dve.tensor_tensor(match, match, cid[:, hs, :].unsqueeze(2).to_broadcast([P, 4, TOPK, CAND]), ALU.mult))
                    wait()
                    did(dve.tensor_reduce(posf[:, hs, :], match, AX.X, ALU.add))
                    wait()
                did(dve.tensor_copy(idi[:, 0, :], posf[:, :, :].rearrange("p h k -> p (h k)")))
                wait()
                did(dve.tensor_scalar(idi[:, 1, :], idi[:, 0, :], 7, None, ALU.arith_shift_right))
                did(dve.tensor_scalar(idi[:, 2, :], idi[:, 0, :], NK - 1, None, ALU.bitwise_and))
                wait()
                did(dve.tensor_copy(found[:, t, 0:2, :], idi[:, 1:3, :]))
                wait()
                if n_dots:
                    dve.wait_ge(dotted[(DOTS_1 + n_dots - 1) % U_RING], DOTS_T // U_RING * (t - 1) + (DOTS_1 + n_dots - 1) // U_RING + 1)
                    did(dve.tensor_copy(dots[:, bass.ds(t * DOTS_T + (DOTS_1 - DOTS_T), DOTS_T)], dot_slot[:, 0:DOTS_T]))
                else:
                    did(dve.memset(dots[:, :], 0.0))
                wait()
                assert me.count[id(dve_line)] == OPS, me.count[id(dve_line)]

            retrieve(0, 0)
            dve.tensor_copy(u_row[:, :], idi[:, 0, :]).then_inc(rows_known, 1)
            dve.scalar_tensor_tensor(v_row[:, :], found[:, 0, 1, :], float(NK), found[:, 0, 0, :], ALU.mult, ALU.add).then_inc(rows_known, 1)
            dve.wait_ge(rows_known, 2)
            for k in range(DOTS_1):
                dot(k % U_RING, 1, k)
            dve.wait_ge(dotted[(DOTS_1 - 1) % U_RING], 1)
            dve.tensor_copy(dots[:, 0:DOTS_1], dot_slot[:, 0:DOTS_1]).then_inc(rows_known, 1)
            dve.wait_ge(rows_known, 3)
            with dve.Fori(1, TB) as t:
                retrieve(t, DOTS_T)
            done = TB * OPS

            def step(ins):
                nonlocal done
                ins.then_inc(dve_line, 1)
                done += 1
                dve.wait_ge(dve_line, done)

            c0 = DOTS_1 + (TB - 1) * DOTS_T
            dve.wait_ge(exp_ready, 1)
            e3 = found[:, :, 2, :].rearrange("p t (h k) -> p t h k", h=PH)
            z2 = zsum[:, :, :].rearrange("p a (t h) -> p a t h", t=TB)
            step(dve.tensor_reduce(z2[:, 0, :, :], e3, AX.X, ALU.add))
            step(dve.reciprocal(zsum[:, 1, :], zsum[:, 0, :]))
            dve.tensor_tensor(e3, e3, spread_last(z2[:, 1, :, :], TOPK), ALU.mult).then_inc(found_ready, 1)
            dve.wait_ge(turned, 1)
            for j in range(3):
                ins = dve.tensor_copy(pair[:, j, :], psG[:, j // 2, j % 2, 0:TB - 1, :].rearrange("p a b -> p (a b)"))
                ins.then_inc(turned_copied, 1)
            dve.wait_ge(turned_copied, 3)
            iota3 = iota.unsqueeze(1).to_broadcast([P, STEP_TOK, P])

            def spread(j):
                n = 0
                for k in range(8):
                    par = k % 2
                    tok = lambda a: spread_last(pair[:, a, bass.ds(j * (8 * STEP_TOK) + k * STEP_TOK, STEP_TOK)], P)
                    reached(dve, gates_summed[par], 4 * j + k // 2)
                    first = dve.tensor_tensor(onehot[:, par, 0, :, :], iota3, tok(0), ALU.is_equal)
                    first.then_inc(dve_line, 1)
                    dve.wait_ge(dve_line, 17 * j + (done + 2 * k + 1))
                    dve.tensor_tensor(onehot[:, par, 0, :, :], onehot[:, par, 0, :, :], tok(2), ALU.mult).then_inc(dve_line, 1)
                    dve.tensor_tensor(onehot[:, par, 1, :, :], iota3, tok(1), ALU.is_equal).then_inc(spread_ready[par], 1)
                    for _ in range(2 - par):
                        c = c0 + n
                        dot(c % U_RING, DOTS_J // U_RING * j + c // U_RING + 1, n)
                        n += 1
                dve.wait_ge(dotted[c % U_RING], DOTS_J // U_RING * j + c // U_RING + 1)
                dve.tensor_copy(dots[:, bass.ds(j * DOTS_J + c0, DOTS_J)], dot_slot[:, 0:DOTS_J]).then_inc(dve_line, 1)

            spread(0)
            with dve.Fori(1, n_body) as j:
                spread(j)
            done += 17 * n_body
            dve.wait_ge(dve_line, done)
            c0 += DOTS_J * n_body
            def weights(par, turn):
                dve.wait_ge(in_loaded[par], 32 * turn)
                a4 = a_in[:, par, :, :].rearrange("p i (g t) -> p i g t", t=GT)
                dve.tensor_tensor(a4, a4, g_in[:, par, :, :, :].rearrange("p g i t -> p i g t"), ALU.mult).then_inc(wg_ready[par], 1)

            def low_weights(par, turn):
                dve.wait_ge(whi_ready[par], turn)
                dve.tensor_tensor(w_lo[:, par, :, :], a_in[:, par, :, :], w_hi[:, par, :, :].bitcast(F32), ALU.subtract).then_inc(wlo_ready[par], 1)

            first_ones = PAIRS - c0 - 3
            for c in range(c0, PAIRS):
                if c == c0 + first_ones:
                    weights(0, 1)
                dot(c % U_RING, c // U_RING + 1, c - c0)
            dve.wait_ge(dotted[(PAIRS - 1) % U_RING], (PAIRS - 1) // U_RING + 1)
            dve.tensor_copy(dots[:, c0:PAIRS], dot_slot[:, 0:PAIRS - c0]).then_inc(dots_ready, 1)
            low_weights(0, 1)
            dve.wait_ge(w0_gelu, 1)
            step(dve.tensor_tensor(w0[:, :], w0[:, :], found[:, 0, 2, :], ALU.mult))

            def add_row(g, k):
                dve.wait_ge(vrow_loaded[k], 16 * g + 16)
                if k:
                    dve.wait_ge(vrow_added[k - 1], g + 1)
                else:
                    reached(dve, vrow_added[UR - 1], g)
                dve.scalar_tensor_tensor(h[:, 0, :], vrows[:, k, :], w0[:, bass.ds(g * UR + k, 1)], h[:, 0, :], ALU.mult, ALU.add)\
                    .then_inc(vrow_added[k], 1)

            def group(g, par, turn, final=False):
                if not final:
                    weights(par, turn)
                add_row(g, 0)
                add_row(g, 1)
                if not final:
                    low_weights(par, turn)
                add_row(g, 2)
                add_row(g, 3)

            dve.wait_ge(h0_loaded, 16)
            group(0, 1, 1)
            with dve.Fori(1, turns // 2) as i:
                group(2 * i - 1, 0, i + 1)
                group(2 * i, 1, i + 1)
            group(turns - 1, 0, 0, final=True)
            dve.wait_ge(tile_used[UR - 1], 2 * turns)
            dve.wait_ge(h_loaded, 16 * (TB - 1))
            for o in range(OUTS):
                hv = h[:, 1 + o // 2, (o % 2) * 512:(o % 2) * 512 + 512]
                dve.tensor_tensor(hv, hv, outs[o], ALU.add).then_inc(h_added, 1)
    new_sem.free()


def embedding(nc, shared, io, out):
    h, con, cols = (shared[k] for k in ("h", "con", "cols"))
    PC = PLE // P
    new_sem = Semaphores(nc)
    with ExitStack() as ctx:
        sb = lambda n, s, d=F32: ctx.enter_context(nc.sbuf_tensor(n, s, d))
        names = ["p_loaded", "g_loaded", "pT_ready", "e_ready", "e_scaled", "sumsq_ready", "ms_ready", "root_ready", "xn_ready",
                 "high_ready", "nT_ready", "gate_ready", "added", "stored", "pe_tile", "act_line", "dve_line", "wp_loaded"]
        sem = {n: new_sem("e_" + n) for n in names}
        psum = ctx.enter_context(nc.psum_tensor("e_psum", [P, 8, 512], F32))
        tiles = [(("pT", c), "pT_ready", c + 1) for c in range(PC)]
        tiles += [(("e", i), "e_ready", 2 * i + 2) for i in range(2 * TB)]
        tiles += [(("nT", c), "nT_ready", c + 1) for c in range(DC)]
        tiles += [(("g", i), "gate_ready", i + 1) for i in range(4 * TB)]
        bank = Banks(psum, tiles, sem, sem["pe_tile"])
        weights = Weights(sb, new_sem, "e", 4)
        wp = sb("e_wp", [P, PC, D])
        pin = sb("e_p", [P, TB, PLE])
        pT = sb("e_pT", [P, PC, T])
        e = sb("e_e", [P, TB, D])
        xn = sb("e_xn", [P, TB, D])
        nT_hi = sb("e_nT_hi", [P, DC, T], F32R)
        nT_lo = sb("e_nT_lo", [P, DC, T], F32R)
        nT = (nT_hi, nT_lo)
        gain = sb("e_gain", [P, D])
        gate = sb("e_gate", [P, 4 * TB, 256])
        junk = sb("e_junk", [P, 512])
        st = sb("e_st", [P, 8, 8])
        ident = con[:, K_ID:K_ID + P]
        block = ctx.enter_context(nc.Block())

        @block.sync
        def _(sp):
            sp.dma_start(pin[:, :, :], io["p"].rearrange("(t p) d -> p t d", p=P)).then_inc(sem["p_loaded"], 16)
            sp.dma_start(wp[:, :, :], io["w_ple"].rearrange("p (c n) -> p c n", c=PC)).then_inc(sem["wp_loaded"], 16)
            sp.dma_start(gain[:, :], io["ple_gain"]).then_inc(sem["g_loaded"], 16)
            for n in range(4):
                weights.load(sp, n, io["w_gate"][n])
            for half in range(2):
                for t in range(TB):
                    sp.wait_ge(sem["added"], (2 * half + 1) * TB + t + 1)
                    sp.dma_start(out[t * P:(t + 1) * P, half * 512:(half + 1) * 512], h[:, t, half * 512:(half + 1) * 512])\
                        .then_inc(sem["stored"], 16)
            sp.wait_ge(sem["stored"], 16 * 2 * TB)

        @block.gpsimd
        def _(pool):
            weights.cut(pool)

        @block.tensor
        def _(pe):
            pe.wait_ge(sem["p_loaded"], 16)
            for c in range(PC):
                out_ = bank.take(pe, "pT", c)
                for t in range(TB):
                    last = pe.transpose(out_[:, t * P:(t + 1) * P], pin[:, t, c * P:(c + 1) * P], ident)
                last.then_inc(sem["pe_tile"], 1)
            pe.wait_ge(sem["pT_ready"], PC)
            pe.wait_ge(sem["wp_loaded"], 16)
            for i in range(2 * TB):
                t, half = i // 2, i % 2
                out_ = bank.take(pe, "e", i)
                for c in range(PC):
                    last = pe.matmul(out_, pT[:, c, t * P:(t + 1) * P], wp[:, c, half * 512:(half + 1) * 512], start=(c == 0), stop=(c == PC - 1))
                last.then_inc(sem["pe_tile"], 1)
            turn_blocks(pe, bank, "nT", sem["xn_ready"], 1, lambda t, c: xn[:, t, c * P:(c + 1) * P], ident)
            for n in range(4):
                w = weights.ready(pe, n)
                for t in range(TB):
                    out_ = bank.take(pe, "g", n * TB + t)[:, 0:256]
                    last = product(pe, out_, lambda part, d: nT[part][:, d, t * P:(t + 1) * P], lambda part, d: w[part][:, d, :],
                                   made=(sem["nT_ready"], 0) if n == t == 0 else None)
                    last.then_inc(sem["pe_tile"], 1)
                pe.drain().then_inc(weights.used[n % 2], 1)

        @block.scalar
        def _(act):
            me = Line(act, sem["act_line"])
            for t in range(TB // 2):
                me.did(act.activation(xn[:, t, :], h[:, t, :], ACT.Square, accum_out=st[:, 0, t:t + 1]), sem["sumsq_ready"])
            act.wait_ge(sem["ms_ready"], 1)
            me.did(act.activation(st[:, 2, 0:TB], st[:, 1, 0:TB], ACT.Sqrt), sem["root_ready"])
            for c in range(PC):
                src = bank.filled(act, "pT", c)
                me.did(act.copy(pT[:, c, :], src), sem["pT_ready"])
            for i in range(2 * TB):
                t, half = i // 2, i % 2
                src = bank.filled(act, "e", i)
                me.did(act.copy(e[:, t, half * 512:(half + 1) * 512], src), sem["e_ready"])
                me.settle()
                me.did(act.activation(junk[:, :], src, ACT.Square, accum_out=st[:, 4, i:i + 1]), sem["e_ready"])
            act.wait_ge(sem["ms_ready"], 2)
            me.did(act.activation(st[:, 6, 0:TB], st[:, 5, 0:TB], ACT.Sqrt), sem["root_ready"])
            for c in range(DC):
                src = bank.filled(act, "nT", c)
                me.did(act.activation(nT_hi[:, c, :], src, ACT.Copy, scale=col(cols, C_GATE + c)), sem["high_ready"])
            for i in range(4 * TB):
                src = bank.filled(act, "g", i)[:, 0:256]
                me.did(act.activation(gate[:, i, :], src, ACT.Sigmoid), sem["gate_ready"])

        @block.vector
        def _(dve):
            me = Line(dve, sem["dve_line"])

            def step(ins, s=None):
                me.did(ins, s)
                me.settle()

            for t in range(TB // 2, TB):
                me.did(dve.tensor_tensor_reduce(xn[:, t, :], h[:, t, :], h[:, t, :], 1.0, 0.0, ALU.mult, ALU.add, st[:, 0, t:t + 1]), sem["sumsq_ready"])
            dve.wait_ge(sem["sumsq_ready"], TB)
            step(dve.tensor_scalar(st[:, 1, 0:TB], st[:, 0, 0:TB], 1.0 / D, EPS, ALU.mult, ALU.add), sem["ms_ready"])
            dve.wait_ge(sem["root_ready"], 1)
            step(dve.reciprocal(st[:, 3, 0:TB], st[:, 2, 0:TB]))
            for t in range(TB):
                me.did(dve.tensor_scalar(xn[:, t, :], h[:, t, :], st[:, 3, t:t + 1], None, ALU.mult), sem["xn_ready"])
            dve.wait_ge(sem["e_ready"], 4 * TB)
            step(dve.tensor_reduce(st[:, 7, 0:TB], st[:, 4, :].rearrange("p (t a) -> p t a", a=2), AX.X, ALU.add))
            step(dve.tensor_scalar(st[:, 5, 0:TB], st[:, 7, 0:TB], 1.0 / D, EPS, ALU.mult, ALU.add), sem["ms_ready"])
            for c in range(DC):
                dve.wait_ge(sem["high_ready"], c + 1)
                me.did(dve.scalar_tensor_tensor(nT_lo[:, c, :], bank.at("nT", c), col(cols, C_GATE + c), nT_hi[:, c, :].bitcast(F32), ALU.mult, ALU.subtract),
                       sem["nT_ready"])
            dve.wait_ge(sem["root_ready"], 2)
            step(dve.reciprocal(st[:, 7, 4:8], st[:, 6, 0:TB]))
            dve.wait_ge(sem["g_loaded"], 16)
            for t in range(TB):
                me.did(dve.scalar_tensor_tensor(e[:, t, :], e[:, t, :], st[:, 7, 4 + t:5 + t], gain[:, :], ALU.mult, ALU.mult))
            me.settle()
            for i in range(4 * TB):
                n, t = i // TB, i % TB
                dve.wait_ge(sem["gate_ready"], i + 1)
                step(dve.tensor_tensor(gate[:, i, :], gate[:, i, :], e[:, t, n * 256:(n + 1) * 256], ALU.mult))
                hv = h[:, t, n * 256:(n + 1) * 256]
                me.did(dve.tensor_tensor(hv, hv, gate[:, i, :], ALU.add), sem["added"])
    new_sem.free()


def block_kernel(nc, io, out):
    act_dram = nc.dram_tensor("act_scratch", [NK, P, DT], F32, kind="Internal").ap()
    gate_dram = nc.dram_tensor("gate_scratch", [DT // GT, P, NK, GT], F32, kind="Internal").ap()
    h_dram = nc.dram_tensor("h_scratch", [TB, P, D], F32, kind="Internal").ap()
    with ExitStack() as ctx:
        sb = lambda c, n, s, d=F32: c.enter_context(nc.sbuf_tensor(n, s, d))
        shared = {"h": sb(ctx, "h", [P, TB, D]), "con": sb(ctx, "con", [P, K_END]), "cols": sb(ctx, "cols", [P, C_END])}
        mixer(nc, shared, io)
        with ExitStack() as mid:
            shared["hn_hi"] = sb(mid, "hn_hi", [P, DC, T], F32R)
            shared["hn_lo"] = sb(mid, "hn_lo", [P, DC, T], F32R)
            shared["scores"] = sb(mid, "scores", [P, TB, LISTS, NK])
            retrieval(nc, shared, io, h_dram)
            experts(nc, shared, io, act_dram, gate_dram, h_dram)
        embedding(nc, shared, io, out)


def constants():
    con = np.zeros((P, K_END), np.float32)
    i = np.arange(P)
    con[:, K_ID:K_ID + P] = i[:, None] == i[None, :]
    con[:, K_TRI:K_TRI + P] = i[:, None] <= i[None, :]
    con[:, K_NEG:K_NEG + P] = np.where(i[:, None] > i[None, :], NEG, 0.0)
    con[:, K_IOTA:K_IOTA + P] = i[None, :]
    con[:, K_URO:K_URO + P] = i[None, :] < CHUNK
    con[:, K_NRO:K_NRO + CHUNK] = NEG
    con[:, K_INV:K_INV + HD // 2] = 1.0 / (10000.0 ** (np.arange(0, HD, 2) / HD)).astype(np.float32)
    return con


def by_feature(g):
    g = np.asarray(g)
    n = g.shape[0] // P
    return np.ascontiguousarray(g.reshape(n, P, -1).transpose(1, 0, 2).reshape(P, -1))


def weight_tiles(w, width=Weights.WIDTH):
    return np.ascontiguousarray(np.stack([by_feature(w[:, a:a + width]) for a in range(0, w.shape[1], width)]))


def kernel(**inputs):
    from concourse import bacc
    from concourse.bass_utils import run_bass_kernel_spmd

    a = {k: np.asarray(v) for k, v in inputs.items()}
    one = {k: v[0] for k, v in a.items() if k not in ("x", "positions")}
    w_in = one["w_in"]
    z0, x0, t0, q0 = 0, SSD_W, SSD_W + 1024, SSD_W + 1024 + SSD_H
    cut = [w_in[:, x0:x0 + 1024], w_in[:, q0:q0 + 512], w_in[:, q0 + 1024:q0 + 1536], w_in[:, q0 + 512:q0 + 1024], w_in[:, z0:z0 + 512]]
    line = np.concatenate([one["dt_bias"], one["a_log"], one["d_skip"], one["q_norm_g"], one["k_norm_g"], one["lam_vecs"].reshape(-1),
                           one["diff_norm_g"], one["ssd_norm_g"]])
    arrays = {
        "x": a["x"][0], "positions": a["positions"].reshape(TB, P).T, "p": one["p"][0],
        "consts": constants(),
        "rows": np.ascontiguousarray(np.broadcast_to(line, (P, R_END))),
        "cols": np.concatenate([by_feature(one["norm_mix_g"][:, None]), by_feature(one["norm_ffn_g"][:, None]),
                                by_feature(one["ple_gate_norm_g"][:, None]), by_feature(one["conv_w"].T),
                                by_feature(one["conv_b"][:, None])], axis=1),
        "w_in": weight_tiles(np.concatenate(cut, axis=1)),
        "w_dt": by_feature(w_in[:, t0:q0]),
        "w_out": weight_tiles(one["w_out"]),
        "w_q": weight_tiles(one["peer_wq"]),
        "keys": np.concatenate([one["peer_k1"].T, one["peer_k2"].T], axis=1),
        "u_t": one["peer_u"].reshape(NK, NK, DC, P).transpose(1, 3, 2, 0).reshape(NK, P, DC * P),
        "v_t": one["peer_v"].reshape(NK, NK, D).transpose(1, 0, 2),
        "u_rows": one["peer_u"],
        "ffn_gain": np.broadcast_to(one["norm_ffn_g"], (P, D)),
        "w_ple": by_feature(one["ple_proj"]),
        "ple_gain": np.broadcast_to(one["ple_norm_g"], (P, D)),
        "w_gate": weight_tiles(one["ple_gate_w"]),
    }
    arrays = {f"in_{k}": np.ascontiguousarray(v) for k, v in arrays.items()}
    nc = bacc.Bacc("TRN2", target_bir_lowering=False, num_devices=1)
    io = {k[3:]: nc.dram_tensor(k, v.shape, mybir.dt.from_np(v.dtype), kind="ExternalInput").ap() for k, v in arrays.items()}
    out = nc.dram_tensor("out_h", (T, D), F32, kind="ExternalOutput").ap()
    block_kernel(nc, io, out)
    r = run_bass_kernel_spmd(nc, [arrays], core_ids=[0])
    return r.results[0]["out_h"].reshape(1, T, D)
```
